# Optimizing a Trainium2 kernel written in Bass

```python
import jax, jax.numpy as jnp
from jax import lax
import numpy as np

D_MODEL = 1024
BATCH = 1
SEQ = 1024
DEPTH = 1

CTX_LEN = 256
GRID_W = 64
N_MOD = 9
EPS = 1e-6
D_FF = 2816
ATTN_HEADS = 8
ATTN_KV_HEADS = 2
HEAD_DIM = 64
ROPE_AXIS_DIM = HEAD_DIM // 2
ROPE_THETA = 10000.0
BLOCK_Q = 128
GLA_HEADS = 4
GLA_DK = 64
GLA_DV = 128
GLA_RANK = 16
GLA_GATE_NORM = 16.0
GLA_CHUNK = 64
ATTN_Q_W = ATTN_HEADS * HEAD_DIM
ATTN_KV_W = ATTN_KV_HEADS * HEAD_DIM
GLA_K_W = GLA_HEADS * GLA_DK
GLA_V_W = GLA_HEADS * GLA_DV
N_BRANCH = 2
IN_SIZES = (ATTN_Q_W, ATTN_KV_W, ATTN_KV_W, GLA_K_W, GLA_K_W, GLA_V_W, GLA_V_W, 2 * GLA_RANK, N_BRANCH * D_MODEL)
IN_SPLITS = tuple(int(v) for v in np.cumsum(IN_SIZES)[:-1])
IN_WIDTH = int(sum(IN_SIZES))

kernel_name = "hybrid_gqa_gla_macaron_dit_layer"

def rms_norm(x, g):
    xf = x.astype(jnp.float32)
    y = xf * lax.rsqrt(jnp.mean(xf * xf, axis=-1, keepdims=True) + EPS)
    return y.astype(x.dtype) * g

def modulate(n, shift, scale):
    return n * (1 + scale) + shift

def swiglu(n, w_up, w_down):
    a, b = jnp.split(n @ w_up, 2, axis=-1)
    return (jax.nn.silu(a) * b) @ w_down

def half_ffn(h, mod, i, g, w_up, w_down):
    shift, scale, gate = mod[..., 3 * i, :], mod[..., 3 * i + 1, :], mod[..., 3 * i + 2, :]
    return h + 0.5 * gate * swiglu(modulate(rms_norm(h, g), shift, scale), w_up, w_down)

def axial_rope(T):
    rows = T // GRID_W
    row = jnp.repeat(jnp.arange(rows, dtype=jnp.float32), GRID_W)
    col = jnp.tile(jnp.arange(GRID_W, dtype=jnp.float32), rows)
    freqs = ROPE_THETA ** (-jnp.arange(0, ROPE_AXIS_DIM, 2, dtype=jnp.float32) / ROPE_AXIS_DIM)
    ang = jnp.concatenate([row[:, None] * freqs, col[:, None] * freqs], axis=-1)
    return jnp.cos(ang)[:, None, :], jnp.sin(ang)[:, None, :]

def apply_rope(x, cos, sin):
    xf = x.astype(jnp.float32)
    x1, x2 = xf[..., :HEAD_DIM // 2], xf[..., HEAD_DIM // 2:]
    return jnp.concatenate([x1 * cos - x2 * sin, x1 * sin + x2 * cos], axis=-1).astype(x.dtype)

def attn_heads(part, n_heads, g):
    return rms_norm(part.reshape(*part.shape[:-1], n_heads, HEAD_DIM), g)

def block_attention(q, k, v):
    B, T, Hq, hd = q.shape
    Hkv = k.shape[2]
    G = Hq // Hkv
    nblk = T // BLOCK_Q
    qb = q.reshape(B, nblk, BLOCK_Q, Hkv, G, hd).transpose(1, 0, 3, 4, 2, 5)
    kt = k.transpose(0, 2, 1, 3)
    vt = v.transpose(0, 2, 1, 3)
    scale = hd ** -0.5

    def one_block(qi):
        s = jnp.einsum('bkgqd,bksd->bkgqs', qi, kt).astype(jnp.float32) * scale
        p = jax.nn.softmax(s, axis=-1).astype(vt.dtype)
        return jnp.einsum('bkgqs,bksd->bkgqd', p, vt)

    o = lax.map(one_block, qb)
    return o.transpose(1, 0, 4, 2, 3, 5).reshape(B, T, Hq * hd)

def to_heads(a, n_heads):
    B, T, _ = a.shape
    return a.reshape(B, T, n_heads, -1).transpose(0, 2, 1, 3)

def gla_chunked(q, k, v, log_a, s0):
    dtype = v.dtype
    q, k, v, log_a = (a.astype(jnp.float32) for a in (q, k, v, log_a))
    B, H, T, dk = q.shape
    dv = v.shape[-1]
    n = T // GLA_CHUNK

    def to_chunks(a):
        return jnp.moveaxis(a.reshape(B, H, n, GLA_CHUNK, a.shape[-1]), 2, 0)

    idx = jnp.arange(GLA_CHUNK)
    lower = (idx[:, None] >= idx[None, :])[:, :, None]

    def step(s, inp):
        qi, ki, vi, gi = inp
        b = jnp.cumsum(gi, axis=2)
        o_inter = jnp.einsum('bhcd,bhde->bhce', qi * jnp.exp(b), s)
        diff = b[:, :, :, None, :] - b[:, :, None, :, :]
        decay = jnp.exp(jnp.where(lower, diff, -jnp.inf))
        A = jnp.einsum('bhid,bhjd,bhijd->bhij', qi, ki, decay)
        o_intra = jnp.einsum('bhij,bhje->bhie', A, vi)
        b_last = b[:, :, -1, :]
        s_new = jnp.exp(b_last)[..., None] * s + jnp.einsum(
            'bhcd,bhce->bhde', ki * jnp.exp(b_last[:, :, None, :] - b), vi)
        return s_new, o_inter + o_intra

    s_fin, o = lax.scan(step, s0, (to_chunks(q), to_chunks(k), to_chunks(v), to_chunks(log_a)))
    o = jnp.moveaxis(o, 0, 2).reshape(B, H, T, dv)
    return o.astype(dtype), s_fin

def gla_bidirectional(parts, w_dec, b_dec, s0_f, s0_b):
    gq = to_heads(parts[3], GLA_HEADS) * (GLA_DK ** -0.5)
    gk = to_heads(parts[4], GLA_HEADS)
    gv = to_heads(parts[5], GLA_HEADS)
    low_f, low_b = jnp.split(parts[7], 2, axis=-1)
    la_f = to_heads(jax.nn.log_sigmoid((low_f @ w_dec[0] + b_dec[0]).astype(jnp.float32)) / GLA_GATE_NORM, GLA_HEADS)
    la_b = to_heads(jax.nn.log_sigmoid((low_b @ w_dec[1] + b_dec[1]).astype(jnp.float32)) / GLA_GATE_NORM, GLA_HEADS)
    o_f, s_f = gla_chunked(gq, gk, gv, la_f, s0_f)
    flip = lambda a: jnp.flip(a, axis=2)
    o_b, s_b = gla_chunked(flip(gq), flip(gk), flip(gv), flip(la_b), s0_b)
    return o_f + flip(o_b), s_f, s_b

def merge_branches(parts, attn_o, gla_o, g_gla, w_branch, b_gate, w_out):
    B, H, T, _ = gla_o.shape
    gla_o = rms_norm(gla_o.transpose(0, 2, 1, 3), g_gla).reshape(B, T, GLA_V_W) * jax.nn.silu(parts[6])
    y_attn = attn_o @ w_branch[0]
    y_gla = gla_o @ w_branch[1]
    g_attn, g_gla_b = jnp.split(jax.nn.sigmoid(parts[8] + b_gate), 2, axis=-1)
    return (g_attn * y_attn + g_gla_b * y_gla) @ w_out

def setup_inputs(seed: int = 0) -> dict:
    key = jax.random.key(seed)
    ks = jax.random.split(key, 19)

    def nrm(k, shape, scale):
        return jax.random.normal(k, shape, jnp.float32) * scale

    D = D_MODEL
    return {
        "x": nrm(ks[0], (BATCH, SEQ, D), 1.0),
        "c": nrm(ks[1], (BATCH, D), 1.0),
        "ctx": nrm(ks[2], (BATCH, CTX_LEN, D), 1.0),
        "c_ctx": nrm(ks[3], (D,), 1.0),
        "w_mod": nrm(ks[4], (DEPTH, D, N_MOD * D), 0.5 * D ** -0.5),
        "b_mod": nrm(ks[5], (DEPTH, N_MOD * D), 0.02),
        "g_norm": 1.0 + nrm(ks[6], (DEPTH, 3, D), 0.02),
        "w_ffn_up": nrm(ks[7], (DEPTH, 2, D, 2 * D_FF), D ** -0.5),
        "w_ffn_down": nrm(ks[8], (DEPTH, 2, D_FF, D), D_FF ** -0.5),
        "w_in": nrm(ks[9], (DEPTH, D, IN_WIDTH), D ** -0.5),
        "g_q": 1.0 + nrm(ks[10], (DEPTH, HEAD_DIM), 0.02),
        "g_k": 1.0 + nrm(ks[11], (DEPTH, HEAD_DIM), 0.02),
        "w_decay": nrm(ks[12], (DEPTH, 2, GLA_RANK, GLA_K_W), GLA_RANK ** -0.5),
        "b_decay": nrm(ks[13], (DEPTH, 2, GLA_K_W), 0.1),
        "g_gla": 1.0 + nrm(ks[14], (DEPTH, GLA_DV), 0.02),
        "w_branch": nrm(ks[15], (DEPTH, N_BRANCH, ATTN_Q_W, D), ATTN_Q_W ** -0.5),
        "b_gate": nrm(ks[16], (DEPTH, N_BRANCH * D), 0.1),
        "w_out": nrm(ks[17], (DEPTH, D, D), D ** -0.5),
        "g_final": 1.0 + nrm(ks[18], (D,), 0.02),
    }

def reference(x, c, ctx, c_ctx, w_mod, b_mod, g_norm, w_ffn_up, w_ffn_down, w_in, g_q, g_k,
              w_decay, b_decay, g_gla, w_branch, b_gate, w_out, g_final):
    B, T, _ = x.shape
    cos, sin = axial_rope(T)
    s_zero = jnp.zeros((B, GLA_HEADS, GLA_DK, GLA_DV), jnp.float32)
    h, hc = x, ctx
    for l in range(DEPTH):
        last = l == DEPTH - 1
        m_lat = (jax.nn.silu(c) @ w_mod[l] + b_mod[l]).reshape(B, 1, N_MOD, D_MODEL)
        m_ctx = (jax.nn.silu(c_ctx) @ w_mod[l] + b_mod[l]).reshape(N_MOD, D_MODEL)

        h = half_ffn(h, m_lat, 0, g_norm[l, 0], w_ffn_up[l, 0], w_ffn_down[l, 0])
        hc = half_ffn(hc, m_ctx, 0, g_norm[l, 0], w_ffn_up[l, 0], w_ffn_down[l, 0])

        n_lat = modulate(rms_norm(h, g_norm[l, 1]), m_lat[..., 3, :], m_lat[..., 4, :])
        n_ctx = modulate(rms_norm(hc, g_norm[l, 1]), m_ctx[3], m_ctx[4])
        p_lat = jnp.split(n_lat @ w_in[l], IN_SPLITS, axis=-1)
        p_ctx = jnp.split(n_ctx @ w_in[l], IN_SPLITS, axis=-1)

        k_ctx = attn_heads(p_ctx[1], ATTN_KV_HEADS, g_k[l])
        v_ctx = p_ctx[2].reshape(*p_ctx[2].shape[:-1], ATTN_KV_HEADS, HEAD_DIM)
        q_lat = apply_rope(attn_heads(p_lat[0], ATTN_HEADS, g_q[l]), cos, sin)
        k_lat = apply_rope(attn_heads(p_lat[1], ATTN_KV_HEADS, g_k[l]), cos, sin)
        v_lat = p_lat[2].reshape(B, T, ATTN_KV_HEADS, HEAD_DIM)
        attn_lat = block_attention(q_lat, jnp.concatenate([k_lat, k_ctx], axis=1),
                                   jnp.concatenate([v_lat, v_ctx], axis=1))

        gla_ctx, s_f, s_b = gla_bidirectional(p_ctx, w_decay[l], b_decay[l], s_zero, s_zero)
        gla_lat, _, _ = gla_bidirectional(p_lat, w_decay[l], b_decay[l], s_f, s_b)

        h = h + m_lat[..., 5, :] * merge_branches(p_lat, attn_lat, gla_lat, g_gla[l], w_branch[l], b_gate[l], w_out[l])

        if not last:
            q_ctx = attn_heads(p_ctx[0], ATTN_HEADS, g_q[l])
            attn_ctx = block_attention(q_ctx, k_ctx, v_ctx)
            hc = hc + m_ctx[5] * merge_branches(p_ctx, attn_ctx, gla_ctx, g_gla[l], w_branch[l], b_gate[l], w_out[l])
            hc = half_ffn(hc, m_ctx, 2, g_norm[l, 2], w_ffn_up[l, 1], w_ffn_down[l, 1])

        h = half_ffn(h, m_lat, 2, g_norm[l, 2], w_ffn_up[l, 1], w_ffn_down[l, 1])
    return rms_norm(h, g_final)


_drawn_inputs = setup_inputs


def setup_inputs(seed=0):
    import zlib

    import numpy as np

    out = dict(_drawn_inputs(seed))
    spreads = {}
    factors = {'ctx': 5.422,
     'c_ctx': 4.585,
     'b_mod': 3.422,
     'g_norm': 8.0,
     'g_q': 8.0,
     'g_k': 8.0,
     'w_decay': 2.808,
     'b_decay': 8.0,
     'g_gla': 8.0,
     'b_gate': 8.0,
     'g_final': 2.904}
    for name, (base, spread) in spreads.items():
        noise = np.random.default_rng([zlib.crc32(name.encode()), seed]).standard_normal(out[name].shape)
        drawn = base * np.exp(spread * noise) if base else spread * noise
        out[name] = __import__('jax').numpy.asarray(drawn.astype(out[name].dtype))
    for name, factor in factors.items():
        out[name] = (out[name] * factor).astype(out[name].dtype)
    return out
```

```python
from contextlib import ExitStack

import concourse.bass as bass
from concourse import mybir
import numpy as np

F32 = mybir.dt.float32
F32R = mybir.dt.float32r
I32 = mybir.dt.int32
ALU = mybir.AluOpType
ACT = mybir.ActivationFunctionType
AX_X = mybir.AxisListType.X

P = 128
D = 1024
KT = D // P
SEQ = 1024
CTX = 256
TOK = SEQ + CTX
D_FF = 2816
EPS = 1e-6
HEADS, KV_HEADS, HD = 8, 2, 64
GLA_HEADS, DK, DV = 4, 64, 128
RANK = 16
GATE_NORM = 16.0
GRID_W = 64
ROPE_THETA = 10000.0
SCALE = HD ** -0.5

LAT = [(0, 512), (512, 512)]
ALL = LAT + [(1024, 256)]

C_Q, C_K, C_V = 0, 512, 640
C_GQ, C_GK, C_GV, C_GZ, C_LOW, C_GATE = 768, 1024, 1280, 1792, 2304, 2336

A_BMOD, A_GNORM, A_GFINAL, A_BGATE, A_C = 0, 72, 96, 104, 120
B_CCTX, B_BDEC, B_GGLA, B_GQ, B_GK = 0, 8, 12, 13, 14
B_ROWS = 15

N_LEVELS = 7
K_ID, K_ONES, K_BLK, K_PERM, K_MASK = 0, 1, 2, 3, 4
N_CONST = K_MASK + N_LEVELS

PANEL0 = 2
CHUNK = 128
N_CHUNKS = TOK // CHUNK
LAT_CHUNKS = SEQ // CHUNK



def shape_constants():
    c = np.zeros((P, N_CONST, P), np.float32)
    i = np.arange(P)
    c[i, K_ID, i] = 1
    c[:, K_ONES] = 1
    c[:, K_BLK] = (i[:, None] // HD == i[None, :] // HD)
    c[i, K_PERM, i ^ (HD // 2)] = 1
    for n in range(N_LEVELS):
        half = CHUNK >> (n + 1)
        same = i[:, None] // (2 * half) == i[None, :] // (2 * half)
        other = (i[:, None] // half) != (i[None, :] // half)
        c[:, K_MASK + n] = same & other
    return c.reshape(P, N_CONST * P)


def rope_tables():
    axis = HD // 2
    freqs = np.float32(ROPE_THETA) ** (-np.arange(0, axis, 2, dtype=np.float32) / np.float32(axis))
    t = np.arange(SEQ)
    row, col = (t // GRID_W).astype(np.float32), (t % GRID_W).astype(np.float32)
    ang = np.concatenate([row[:, None] * freqs, col[:, None] * freqs], axis=-1).astype(np.float32)
    d = np.arange(P)
    sign = np.where(d % HD < HD // 2, -1, 1).astype(np.float32)
    cos, sin = np.cos(ang).T, np.sin(ang).T
    return np.stack([cos[d % axis], sin[d % axis] * sign[:, None]]).astype(np.float32)


def build(nc, x, c, ctx_in, c_ctx, w_mod, b_mod, g_norm, w_ffn_up, w_ffn_down, w_in, g_q, g_k,
          w_decay, b_decay, g_gla, w_branch, b_gate, w_out, g_final, consts, rope, out):
    stack = ExitStack()
    base = 16512

    def at(name, kb, shape, dt=F32):
        return nc.alloc_sbuf_tensor_at(name, [P, *shape], dt, offset=base + int(kb * 1024))

    def sem(name):
        return stack.enter_context(nc.semaphore(name))

    h0 = at("h0", 0, [KT, TOK])
    nh0, nl0 = at("nh0", 40, [KT, TOK], F32R), at("nl0", 80, [KT, TOK], F32R)
    x_rows = at("x_rows", 40, [TOK // P, D])
    mod_raw = at("mod_raw", 120, [4, KT, P])
    hidh0, hidl0 = at("hidh0", 120, [2, TOK], F32R), at("hidl0", 130, [2, TOK], F32R)
    raw = at("raw", 140, [2, 1024])
    wh, wl = at("wh", 148, [2, 1024], F32R), at("wl", 156, [2, 1024], F32R)
    silu_a = at("silu_a", 164, [3, 512])
    prod = at("prod", 170, [2, 512])
    sq = at("sq", 174, [2, 512])
    rstd = at("rstd", 178, [TOK])
    cols_a, cols_b = at("cols_a", 183, [P]), at("cols_b", 183.5, [16])
    modv = at("modv", 184, [72, 2])
    coef = at("coef", 184.75, [3, KT, 2])
    gates = at("gates", 185, [3, KT, 2])
    silu_c = at("silu_c", 185.25, [KT, 2])
    cst = at("cst", 185.5, [N_CONST, P])
    vec_a, vec_b = at("vec_a", 193, [P]), at("vec_b", 193.5, [P])
    norm_t, norm_f = at("norm_t", 193, [2, 512]), at("norm_f", 197, [2, 512])
    y_rows = at("y_rows", 104, [2, D])
    h1 = at("h1", 40, [KT, SEQ])
    n1h, n1l = at("n1h", 0, [KT, SEQ], F32R), at("n1l", 72, [KT, SEQ], F32R)
    hidh1, hidl1 = at("hidh1", 120, [2, SEQ], F32R), at("hidl1", 128, [2, SEQ], F32R)
    y_fin = at("y_fin", 0, [KT, SEQ])

    ident = cst[:, K_ID, :]
    ones = cst[:, K_ONES, :]

    ps = [stack.enter_context(nc.psum_tensor(f"ps{i}", [P, 512], F32)) for i in range(8)]

    raw_loaded = [sem("raw_loaded0"), sem("raw_loaded1")]
    panel_split = sem("panel_split")
    panel_used = sem("panel_used")
    vec_loaded = sem("vec_loaded")
    const_loaded = sem("const_loaded")
    rows_loaded = [sem(f"rows_loaded{i}") for i in range(TOK // P)]
    cols_ready = sem("cols_ready")
    cols_copied = sem("cols_copied")
    turned = sem("turned")
    turn_evac_v, turn_evac_s = sem("turn_evac_v"), sem("turn_evac_s")
    silu_c_done = sem("silu_c_done")
    mod_loaded = [sem(f"mod_loaded{i}") for i in range(4)]
    mod_product = sem("mod_product")
    mod_evac = sem("mod_evac")
    coef_done = sem("coef_done")
    out_stored = [sem("out_stored0"), sem("out_stored1")]
    fin_turned, fin_evac_v, fin_evac_s = sem("fin_turned"), sem("fin_evac_v"), sem("fin_evac_s")
    n_mod = 72

    def split_panel(dve, p, n=1024):
        q, par = p
        dve.wait_ge(raw_loaded[par], 16 * q)
        dve.wait_ge(panel_used, 2 * q + par - 1)
        nc.vector.tensor_copy(wh[:, par, 0:n], raw[:, par, 0:n]).then_inc(panel_split, 1)
        dve.wait_ge(panel_split, 4 * q + 2 * par + 1)
        nc.vector.tensor_tensor(wl[:, par, 0:n], raw[:, par, 0:n], wh[:, par, 0:n].bitcast(F32),
                                ALU.subtract).then_inc(panel_split, 1)

    def pn(p):
        return (p // 2, p % 2)

    def load_panel(sp, p, dst, src):
        q, par = p
        sp.wait_ge(panel_split, 4 * q + 2 * par - 2)
        sp.dma_start(dst, src).then_inc(raw_loaded[par], 16)

    def wait_panel(pe, p):
        q, par = p
        pe.wait_ge(panel_split, 4 * q + 2 * par + 2)

    def three(pe, o, hi_w, lo_w, hi_x, lo_x, first, last):
        pe.matmul(o, hi_w, hi_x, start=first, stop=False)
        pe.matmul(o, hi_w, lo_x, start=False, stop=False)
        return pe.matmul(o, lo_w, hi_x, start=False, stop=last)

    def load_sp(sp):
        rows = lambda a: a.rearrange("(r c) -> r c", c=P)
        vec = [
            (vec_a[A_BMOD:A_BMOD + 72, :], rows(b_mod[0])),
            (vec_a[A_GNORM:A_GNORM + 24, :], g_norm[0].rearrange("i (r c) -> (i r) c", c=P)),
            (vec_a[A_GFINAL:A_GFINAL + 8, :], rows(g_final)),
            (vec_a[A_BGATE:A_BGATE + 16, :], rows(b_gate[0])),
            (vec_a[A_C:A_C + 8, :], rows(c[0])),
            (vec_b[B_CCTX:B_CCTX + 8, :], rows(c_ctx)),
            (vec_b[B_BDEC:B_BDEC + 4, :], b_decay[0].rearrange("i (r c) -> (i r) c", c=P)),
            (vec_b[B_GGLA:B_GGLA + 1, :], g_gla),
            (vec_b[B_GQ:B_GQ + 1, 0:HD], g_q), (vec_b[B_GQ:B_GQ + 1, HD:P], g_q),
            (vec_b[B_GK:B_GK + 1, 0:HD], g_k), (vec_b[B_GK:B_GK + 1, HD:P], g_k),
        ]
        sp.dma_start(cst[:, :, :], consts.rearrange("p (n c) -> p n c", c=P)).then_inc(const_loaded, 16)
        for dst, src in vec:
            sp.dma_start(dst, src).then_inc(vec_loaded, 16)
        for i in range(TOK // P):
            src = x[0, i * P:(i + 1) * P, :] if i < SEQ // P else ctx_in[0, i * P - SEQ:(i + 1) * P - SEQ, :]
            sp.dma_start(x_rows[:, i, :], src).then_inc(rows_loaded[i], 16)
        mod_v = w_mod[0].rearrange("(k p) n -> p k n", p=P)
        for p in range(n_mod):
            if p >= 4:
                sp.wait_ge(mod_product, p - 3)
            sp.dma_start(mod_raw[:, p % 4, :, :], mod_v[:, :, p * P:(p + 1) * P]).then_inc(mod_loaded[p % 4], 16)

    N_VEC_DMA = 12

    def load_pe(pe):
        pe.wait_ge(const_loaded, 16)
        pe.wait_ge(vec_loaded, 16 * N_VEC_DMA)
        pe.transpose(ps[7][:, 0:P], vec_a[:, :], ident).then_inc(cols_ready, 1)
        pe.transpose(ps[7][:, P:P + B_ROWS], vec_b[0:B_ROWS, :], ident[0:B_ROWS, 0:B_ROWS]).then_inc(cols_ready, 1)
        for i in range(TOK // P):
            pe.wait_ge(rows_loaded[i], 16)
            for q in range(2):
                u = 2 * i + q
                if u >= 6:
                    pe.wait_ge(turn_evac_s if q else turn_evac_v, (u - 6) // 2 + 1)
                for k in range(4):
                    mm = pe.transpose(ps[u % 6][:, k * P:(k + 1) * P],
                                      x_rows[:, i, (4 * q + k) * P:(4 * q + k + 1) * P], ident)
                mm.then_inc(turned, 1)
        pe.wait_ge(silu_c_done, 2)
        pe.wait_ge(cols_copied, 2)
        for p in range(n_mod):
            b = p // 8
            if p % 8 == 0 and b >= 2:
                pe.wait_ge(mod_evac, b - 1)
            pe.wait_ge(mod_loaded[p % 4], 16 * (p // 4 + 1))
            for k in range(KT):
                mm = pe.matmul(ps[6 + b % 2][:, 2 * (p % 8):2 * (p % 8) + 2], mod_raw[:, p % 4, k, :],
                               silu_c[:, k, :], start=(k == 0), stop=(k == KT - 1))
            mm.then_inc(mod_product, 1)

    def turn_evac(nc_copy, q, done):
        for i in range(TOK // P):
            u = 2 * i + q
            nc_copy(u, h0[:, 4 * q:4 * q + 4, i * P:(i + 1) * P],
                    ps[u % 6][:, :].rearrange("p (k t) -> p k t", k=4)).then_inc(done, 1)

    def load_act(act):
        act.wait_ge(cols_copied, 2)
        nc.scalar.activation(silu_c[:, :, 0], cols_a[:, A_C:A_C + 8], ACT.Silu).then_inc(silu_c_done, 1)
        nc.scalar.activation(silu_c[:, :, 1], cols_b[:, B_CCTX:B_CCTX + 8], ACT.Silu).then_inc(silu_c_done, 1)

        def copy(u, o, i):
            act.wait_ge(turned, u + 1)
            return nc.scalar.activation(o, i, ACT.Copy)
        turn_evac(copy, 1, turn_evac_s)

    def load_dve(dve):
        dve.wait_ge(cols_ready, 2)
        nc.vector.tensor_copy(cols_a[:, :], ps[7][:, 0:P]).then_inc(cols_copied, 1)
        nc.vector.tensor_copy(cols_b[:, 0:B_ROWS], ps[7][:, P:P + B_ROWS]).then_inc(cols_copied, 1)

        def copy(u, o, i):
            dve.wait_ge(turned, u + 1)
            return nc.vector.tensor_copy(o, i)
        turn_evac(copy, 0, turn_evac_v)
        dve.wait_ge(cols_copied, 2)
        for b in range(n_mod // 8):
            dve.wait_ge(mod_product, 8 * (b + 1))
            nc.vector.tensor_tensor(modv[:, 8 * b:8 * b + 8, :],
                                    ps[6 + b % 2][:, 0:16].rearrange("p (n s) -> p n s", s=2),
                                    cols_a[:, A_BMOD + 8 * b:A_BMOD + 8 * b + 8].unsqueeze(2)
                                    .to_broadcast([P, 8, 2]), ALU.add).then_inc(mod_evac, 1)
            if b % 3 == 2:
                i = b // 3
                dve.wait_ge(mod_evac, b + 1)
                nc.vector.scalar_tensor_tensor(
                    coef[:, i, :, :], modv[:, 8 * (3 * i + 1):8 * (3 * i + 2), :], 1.0,
                    cols_a[:, A_GNORM + 8 * i:A_GNORM + 8 * i + 8].unsqueeze(2).to_broadcast([P, 8, 2]),
                    ALU.add, ALU.mult).then_inc(coef_done, 1)
                nc.vector.tensor_scalar(gates[:, i, :, :], modv[:, 8 * (3 * i + 2):8 * (3 * i + 3), :],
                                        1.0 if i == 1 else 0.5, None, ALU.mult).then_inc(coef_done, 1)

    class Norm:
        sq_done, sq_used = sem("sq_done"), sem("sq_used")
        ms_done, root_done, rstd_done = sem("ms_done"), sem("root_done"), sem("rstd_done")
        scaled, plain_done, hi_done, lo_done = sem("scaled"), sem("plain_done"), sem("hi_done"), sem("lo_done")

        def __init__(self, c0, i, h, hi, lo, chunks, final=None):
            self.i, self.h, self.hi, self.lo, self.chunks, self.final = i, h, hi, lo, chunks, final
            self.c0, self.u0 = c0, KT * c0

        def normed(self, eng, c):
            eng.wait_ge(self.lo_done, self.u0 + KT * (c + 1))

        def act(self, act, ready):
            def squares(c):
                t0, w = self.chunks[c]
                for k in range(KT):
                    u = c * KT + k
                    ready(act, c, k)
                    if u >= 2:
                        act.wait_ge(self.sq_used, self.u0 + u - 1)
                    nc.scalar.activation(sq[:, u % 2, 0:w], self.h[:, k, t0:t0 + w], ACT.Square)\
                        .then_inc(self.sq_done, 1)
            squares(0)
            for c, (t0, w) in enumerate(self.chunks):
                if c + 1 < len(self.chunks):
                    squares(c + 1)
                act.wait_ge(self.ms_done, self.c0 + c + 1)
                nc.scalar.activation(rstd[:, t0:t0 + w], rstd[:, t0:t0 + w], ACT.Sqrt).then_inc(self.root_done, 1)
                if self.final is not None:
                    continue
                s = 1 if t0 >= SEQ else 0
                for k in range(KT):
                    u = c * KT + k
                    a, b = coef[:, self.i, k, s:s + 1], modv[:, 8 * 3 * self.i + k, s:s + 1]
                    act.wait_ge(self.scaled, self.u0 + u + 1)
                    if u >= 2:
                        act.wait_ge(self.lo_done, self.u0 + u - 1)
                    nc.scalar.activation(norm_f[:, u % 2, 0:w], norm_t[:, u % 2, 0:w], ACT.Identity,
                                         bias=b, scale=a).then_inc(self.plain_done, 1)
                    nc.scalar.activation(self.hi[:, k, t0:t0 + w], norm_t[:, u % 2, 0:w], ACT.Identity,
                                         bias=b, scale=a).then_inc(self.hi_done, 1)

        def pe(self, pe):
            for c, (t0, w) in enumerate(self.chunks):
                for k in range(KT):
                    u = c * KT + k
                    pe.wait_ge(self.sq_done, self.u0 + u + 1)
                    pe.matmul(ps[c][:, 0:w], ones, sq[:, u % 2, 0:w], start=(k == 0), stop=(k == KT - 1))\
                        .then_inc(self.sq_used, 1)

        def dve(self, dve):
            n = len(self.chunks)

            def lo(u):
                c, k = divmod(u, KT)
                t0, w = self.chunks[c]
                dve.wait_ge(self.hi_done, self.u0 + u + 1)
                nc.vector.tensor_tensor(self.lo[:, k, t0:t0 + w], norm_f[:, u % 2, 0:w],
                                        self.hi[:, k, t0:t0 + w].bitcast(F32), ALU.subtract)\
                    .then_inc(self.lo_done, 1)
            for c, (t0, w) in enumerate(self.chunks):
                dve.wait_ge(self.sq_used, self.u0 + KT * (c + 1))
                nc.vector.tensor_scalar(rstd[:, t0:t0 + w], ps[c][:, 0:w], 1.0 / D, EPS, ALU.mult, ALU.add)\
                    .then_inc(self.ms_done, 1)
                dve.wait_ge(self.root_done, self.c0 + c + 1)
                nc.vector.reciprocal(rstd[:, t0:t0 + w], rstd[:, t0:t0 + w]).then_inc(self.rstd_done, 1)
                dve.wait_ge(self.rstd_done, self.c0 + c + 1)
                for k in range(KT):
                    u = c * KT + k
                    if self.final is not None:
                        nc.vector.scalar_tensor_tensor(self.final[:, k, t0:t0 + w], self.h[:, k, t0:t0 + w],
                                                       cols_a[:, A_GFINAL + k:A_GFINAL + k + 1],
                                                       rstd[:, t0:t0 + w], ALU.mult, ALU.mult)\
                            .then_inc(self.scaled, 1)
                        continue
                    nc.vector.tensor_tensor(norm_t[:, u % 2, 0:w], self.h[:, k, t0:t0 + w], rstd[:, t0:t0 + w],
                                            ALU.mult).then_inc(self.scaled, 1)
                    if u >= 1:
                        lo(u - 1)
            if self.final is None:
                lo(n * KT - 1)

    class Ffn:
        GROUPS = D_FF // 256

        def __init__(self, tag, f, gate_i, h, norm, hid_hi, hid_lo, chunks, panel0):
            self.f, self.gate_i, self.h, self.norm = f, gate_i, h, norm
            self.hh, self.hl, self.chunks, self.panel0 = hid_hi, hid_lo, chunks, panel0
            self.up_done = sem(f"up_done_{tag}")
            self.a_free = sem(f"a_free_{tag}")
            self.b_free = sem(f"b_free_{tag}")
            self.hid_done = sem(f"hid_done_{tag}")
            self.down_done = sem(f"down_done_{tag}")
            self.down_free = sem(f"down_free_{tag}")
            self.end_panel = panel0 + 6 * self.GROUPS

        def run(self, eng, body):
            with eng.Fori(0, self.GROUPS - 1) as g:
                body(g, False)
            body(self.GROUPS - 1, True)

        def panel(self, g, j):
            return (3 * g + (self.panel0 + j) // 2, (self.panel0 + j) % 2)

        def slot(self, j):
            return (self.panel0 + j) % 2

        def sp(self, sp):
            up = w_ffn_up[0, self.f].rearrange("(k p) n -> p k n", p=P)
            down = w_ffn_down[0, self.f].rearrange("(k p) n -> p k n", p=P)

            def body(g, last):
                for j in range(4):
                    col = g * 256 + (j // 2) * P + (j % 2) * D_FF
                    load_panel(sp, self.panel(g, j), raw[:, self.slot(j), :].rearrange("p (k n) -> p k n", k=KT),
                               up[:, :, bass.ds(col, P)])
                for j in range(4, 6):
                    load_panel(sp, self.panel(g, j), raw[:, self.slot(j), :].rearrange("p (k n) -> p k n", k=2),
                               down[:, bass.ds(g * 2, 2), (j - 4) * 512:(j - 3) * 512])
            self.run(sp, body)

        def pe(self, pe):
            C = len(self.chunks)

            def body(g, last):
                for j in range(4):
                    t, half = j // 2, j % 2
                    wait_panel(pe, self.panel(g, j))
                    for c, (t0, w) in enumerate(self.chunks):
                        if j == 0:
                            self.norm.normed(pe, c)
                        pe.wait_ge(self.b_free if half else self.a_free, g * (2 * C) + (t * C + c + 1))
                        o = ps[c + 3 * half][:, 0:w]
                        for k in range(KT):
                            mm = three(pe, o, wh[:, self.slot(j), k * P:(k + 1) * P],
                                       wl[:, self.slot(j), k * P:(k + 1) * P],
                                       self.norm.hi[:, k, t0:t0 + w], self.norm.lo[:, k, t0:t0 + w],
                                       k == 0, k == KT - 1)
                        mm.then_inc(self.up_done if c < C - 1 else panel_used, 1)
                for j in range(4, 6):
                    wait_panel(pe, self.panel(g, j))
                    for n in range(4):
                        for c, (t0, w) in enumerate(self.chunks):
                            i = ((j - 4) * 4 + n) * C + c
                            if j == 4 and n == 0:
                                pe.wait_ge(self.hid_done, g * (4 * C) + 2 * (C + c) + 2)
                            pe.wait_ge(self.down_free, g * (8 * C) + (i + 1))
                            o = ps[6 + i % 2][:, 0:w]
                            for k in range(2):
                                cols = slice(k * 512 + n * P, k * 512 + (n + 1) * P)
                                mm = three(pe, o, wh[:, self.slot(j), cols], wl[:, self.slot(j), cols],
                                           self.hh[:, k, t0:t0 + w], self.hl[:, k, t0:t0 + w], k == 0, k == 1)
                            mm.then_inc(self.down_done if not (n == 3 and c == C - 1) else panel_used, 1)
            self.run(pe, body)

        def wait_up(self, eng, g, t, half, c):
            C = len(self.chunks)
            if c < C - 1:
                eng.wait_ge(self.up_done, g * (4 * (C - 1)) + ((2 * t + half) * (C - 1) + c + 1))
            else:
                eng.wait_ge(panel_used, g * 6 + (self.panel0 + 2 * t + half + 1))

        def act(self, act):
            C = len(self.chunks)
            act.sem_inc(self.a_free, C)

            def body(g, last):
                for t in range(2):
                    for c, (t0, w) in enumerate(self.chunks):
                        self.wait_up(act, g, t, 0, c)
                        act.wait_ge(self.b_free, g * (2 * C) + (t * C + c + 1))
                        nc.scalar.activation(silu_a[:, c, 0:w], ps[c][:, 0:w], ACT.Silu).then_inc(self.a_free, 1)
            self.run(act, body)

        def dve(self, dve):
            C = len(self.chunks)
            dve.sem_inc(self.b_free, C)
            dve.sem_inc(self.down_free, 2)
            split_panel(dve, pn(self.panel0))

            def hidden(g, t):
                for c, (t0, w) in enumerate(self.chunks):
                    u = t * C + c
                    self.wait_up(dve, g, t, 1, c)
                    dve.wait_ge(self.a_free, g * (2 * C) + (u + C + 1))
                    nc.vector.tensor_tensor(prod[:, c % 2, 0:w], silu_a[:, c, 0:w], ps[3 + c][:, 0:w],
                                            ALU.mult).then_inc(self.b_free, 1)
                    dve.wait_ge(self.b_free, g * (2 * C) + (u + C + 1))
                    nc.vector.tensor_copy(self.hh[:, t, t0:t0 + w], prod[:, c % 2, 0:w]).then_inc(self.hid_done, 1)
                    dve.wait_ge(self.hid_done, g * (4 * C) + (2 * u + 1))
                    nc.vector.tensor_tensor(self.hl[:, t, t0:t0 + w], prod[:, c % 2, 0:w],
                                            self.hh[:, t, t0:t0 + w].bitcast(F32), ALU.subtract)\
                        .then_inc(self.hid_done, 1)

            def residual(g, j):
                for n in range(4):
                    for c, (t0, w) in enumerate(self.chunks):
                        i = ((j - 4) * 4 + n) * C + c
                        if n == 3 and c == C - 1:
                            dve.wait_ge(panel_used, g * 6 + (self.panel0 + j + 1))
                        else:
                            dve.wait_ge(self.down_done, g * (8 * C - 2) + (i - (j - 4) + 1))
                        s = 1 if t0 >= SEQ else 0
                        k = (j - 4) * 4 + n
                        hk = self.h[:, k, t0:t0 + w]
                        nc.vector.scalar_tensor_tensor(hk, ps[6 + i % 2][:, 0:w], gates[:, self.gate_i, k, s:s + 1],
                                                       hk, ALU.mult, ALU.add).then_inc(self.down_free, 1)

            def body(g, last):
                for j in range(6):
                    if not (last and j == 5):
                        split_panel(dve, self.panel(g, j + 1))
                    if j in (1, 3):
                        hidden(g, j // 2)
                    if j >= 4:
                        if j == 4:
                            dve.wait_ge(self.down_free, g * (8 * C) + 2)
                        residual(g, j)
            self.run(dve, body)

        def wait_end(self, eng):
            eng.wait_ge(self.down_free, 2 + 8 * len(self.chunks) * self.GROUPS)

    def result_pe(pe, ready):
        for i in range(SEQ // P):
            ready(pe, i)
            for q in range(2):
                u = 2 * i + q
                if u >= 6:
                    pe.wait_ge(fin_evac_s if q else fin_evac_v, (u - 6) // 2 + 1)
                for k in range(4):
                    mm = pe.transpose(ps[2 + u % 6][:, k * P:(k + 1) * P],
                                      y_fin[:, 4 * q + k, i * P:(i + 1) * P], ident)
                mm.then_inc(fin_turned, 1)

    def result_copy(eng, q, copy, done):
        for i in range(SEQ // P):
            u = 2 * i + q
            eng.wait_ge(fin_turned, u + 1)
            if i >= 2:
                eng.wait_ge(out_stored[i % 2], 16 * (i // 2))
            copy(y_rows[:, i % 2, q * 512:(q + 1) * 512], ps[2 + u % 6][:, :]).then_inc(done, 1)

    def result_sp(sp):
        for i in range(SEQ // P):
            sp.wait_ge(fin_evac_v, i + 1)
            sp.wait_ge(fin_evac_s, i + 1)
            sp.dma_start(out[0, i * P:(i + 1) * P, :], y_rows[:, i % 2, :]).then_inc(out_stored[i % 2], 16)
        for b in range(2):
            sp.wait_ge(out_stored[b], 16 * (SEQ // P // 2))

    gk_f, gv_f = at("gk_f", 0, [2, TOK]), at("gv_f", 10, [4, TOK])
    k_f, v_f = at("k_f", 30, [TOK]), at("v_f", 35, [TOK])
    q_f = at("q_f", 120, [4, SEQ])
    gq_f, low_f = at("gq_f", 193, [2, SEQ]), at("low_f", 201, [TOK])
    staged = at("staged", 164, [4, 512])
    la = at("la", 40, [4, TOK])
    kk = la
    cum = at("cum", 60, [4, TOK])
    vtok = at("vtok", 80, [N_CHUNKS, GLA_HEADS * DV])
    states = at("states", 100, [2, 9, 2, DV])
    lsa, lsb = at("lsa", 140, [2, 512]), at("lsb", 144, [2, 512])
    wdec = at("wdec", 148, [512])
    ktok = at("ktok", 150, [2, 256])
    last = at("last", 152, [4, N_CHUNKS])
    elast = at("elast", 152.5, [4, N_CHUNKS])
    dexp = at("dexp", 154, [2, TOK])
    gla_o = at("gla_o", 10, [GLA_HEADS, SEQ])
    eq, ek = at("eq", 140, [2, 512]), at("ek", 144, [2, 512])
    qc, kc = at("qc", 148, [2, 512]), at("kc", 152, [2, 512])
    scores = at("scores", 156, [2, 4, 2, P])
    qdec = at("qdec", 40, [2, 2, 512])
    gz_s = at("gz_s", 80, [GLA_HEADS, SEQ])
    gla_n = at("gla_n", 164, [2, 512])
    glah, glal = at("glah", 40, [GLA_HEADS, SEQ], F32R), at("glal", 56, [GLA_HEADS, SEQ], F32R)
    rope_t = at("rope_t", 164, [2, SEQ])
    qn, rot = at("qn", 140, [2, 512]), at("rot", 144, [2, 512])
    rot_b = at("rot_b", 148, [2, 512])
    qk_sq = at("qk_sq", 152, [2, 512])
    qk_r = at("qk_r", 156, [2, 512])
    qs = at("qs", 72, [HEADS, SEQ], F32R)
    kh, kl = at("kh", 0, [KV_HEADS, TOK], F32R), at("kl", 10, [KV_HEADS, TOK], F32R)
    vv = at("vv", 20, [TOK // P, KV_HEADS, 2, HD], F32R)
    pth, ptl = at("pth", 140, [TOK // P, 512], F32R), at("ptl", 160, [TOK // P, 512], F32R)
    prob = at("prob", 193, [2, TOK])
    att_t = at("att_t", 30, [4, 512])
    diag = at("diag", 38, [4, P])
    mx, rs = at("mx", 136, [64, 4]), at("rs", 137, [64, 4])
    mtot, nmax = at("mtot", 138, [64]), at("nmax", 138.25, [64])
    rtot, rinv = at("rtot", 138.5, [64]), at("rinv", 138.75, [64])
    ah, al = at("ah", 104, [4, SEQ], F32R), at("al", 120, [4, SEQ], F32R)
    merge_gate = at("merge_gate", 164, [2, 2, SEQ])
    ma, mb = at("ma", 193, [2, 512]), at("mb", 197, [2, 512])
    mh, ml = at("mh", 0, [KT, SEQ], F32R), at("ml", 72, [KT, SEQ], F32R)

    h_dram = nc.dram_tensor("h_saved", (P, KT, SEQ), F32, kind="Internal").ap()
    gate_dram = nc.dram_tensor("gates_saved", (20, P, SEQ), F32, kind="Internal").ap()

    win = [(C_K, P, ALL, lambda t0, w: k_f[:, t0:t0 + w]), (C_V, P, ALL, lambda t0, w: v_f[:, t0:t0 + w])]
    win += [(C_GK + i * P, P, ALL, lambda t0, w, i=i: gk_f[:, i, t0:t0 + w]) for i in range(2)]
    win += [(C_GV + i * P, P, ALL, lambda t0, w, i=i: gv_f[:, i, t0:t0 + w]) for i in range(4)]
    win += [(C_LOW, 2 * RANK, ALL, lambda t0, w: low_f[0:2 * RANK, t0:t0 + w])]
    win += [(C_Q + i * P, P, LAT, lambda t0, w, i=i: q_f[:, i, t0:t0 + w]) for i in range(4)]
    win += [(C_GQ + i * P, P, LAT, lambda t0, w, i=i: gq_f[:, i, t0:t0 + w]) for i in range(2)]
    N_KEPT = len(win)
    win += [(C_GZ + i * P, P, LAT, i) for i in range(4)]
    win += [(C_GATE + i * P, P, LAT, 4 + i) for i in range(16)]
    win_units = [(i, c) for i, (_, _, chunks, _) in enumerate(win) for c in range(len(chunks))]

    win_done, win_evac = sem("win_done"), sem("win_evac")
    saved = [sem(f"saved{i}") for i in range(4)]
    h_saved = sem("h_saved")

    def win_sp(sp, panel0, ffn0, norm):
        ffn0.wait_end(sp)
        sp.dma_start(h_dram, h0[:, :, 0:SEQ]).then_inc(h_saved, 16)
        w = w_in[0].rearrange("(k p) n -> p k n", p=P)
        for i, (col, width, _, _) in enumerate(win):
            p = panel0 + i
            load_panel(sp, pn(p), raw[:, p % 2, 0:KT * width].rearrange("p (k n) -> p k n", k=KT),
                       w[:, :, col:col + width])

    def win_pe(pe, panel0, norm):
        u = 0
        for i, (_, m, chunks, _) in enumerate(win):
            p = panel0 + i
            wait_panel(pe, pn(p))
            for c, (t0, w) in enumerate(chunks):
                if i == 0:
                    norm.normed(pe, c)
                if u >= 8:
                    pe.wait_ge(win_evac, u - 7)
                for k in range(KT):
                    cols = slice(k * m, (k + 1) * m)
                    mm = three(pe, ps[u % 8][0:m, 0:w], wh[:, p % 2, cols], wl[:, p % 2, cols],
                               norm.hi[:, k, t0:t0 + w], norm.lo[:, k, t0:t0 + w], k == 0, k == KT - 1)
                mm.then_inc(win_done if c < len(chunks) - 1 else panel_used, 1)
                u += 1

    def win_act(act, panel0):
        act.wait_ge(h_saved, 16)
        inner, kept = 0, sum(len(ch) for _, _, ch, _ in win[:N_KEPT])
        for u, (i, c) in enumerate(win_units):
            _, m, chunks, target = win[i]
            t0, w = chunks[c]
            if c < len(chunks) - 1:
                inner += 1
                act.wait_ge(win_done, inner)
            else:
                act.wait_ge(panel_used, panel0 + i + 1)
            src = ps[u % 8][0:m, 0:w]
            if i < N_KEPT:
                nc.scalar.activation(target(t0, w), src, ACT.Copy).then_inc(win_evac, 1)
                continue
            n = u - kept
            if n >= 4:
                act.wait_ge(saved[n % 4], 16 * (n // 4))
            if target < 4:
                nc.scalar.activation(staged[:, n % 4, :], src, ACT.Silu).then_inc(win_evac, 1)
            else:
                b = A_BGATE + target - 4
                nc.scalar.activation(staged[:, n % 4, :], src, ACT.Sigmoid, bias=cols_a[:, b:b + 1])\
                    .then_inc(win_evac, 1)
            act.wait_ge(win_evac, u + 1)
            act.dma_start(gate_dram[target, :, t0:t0 + w], staged[:, n % 4, :]).then_inc(saved[n % 4], 16)

    def win_dve(dve, panel0):
        for i, (_, width, _, _) in enumerate(win):
            split_panel(dve, pn(panel0 + i), KT * width)

    dec_loaded = sem("dec_loaded")
    dec_zero = sem("dec_zero")
    g_abs, g_exp, g_ln = sem("g_abs"), sem("g_exp"), sem("g_ln")
    g_logit, g_min, g_la = sem("g_logit"), sem("g_min"), sem("g_la")
    g_scan = sem("g_scan")
    g_last, g_elast, g_diff, g_dexp, g_kk = sem("g_last"), sem("g_elast"), sem("g_diff"), sem("g_dexp"), sem("g_kk")
    g_vt, g_vcopy = sem("g_vt"), sem("g_vcopy")
    g_kt, g_kcopy, g_ds, g_state = sem("g_kt"), sem("g_kcopy"), sem("g_ds"), sem("g_state")
    dec_units = [(j, c) for j in range(4) for c in range(3)]

    def gla_setup_sp(sp):
        sp.wait_ge(dec_zero, 1)
        sp.dma_start(wdec[0:RANK, 0:256], w_decay[0, 0]).then_inc(dec_loaded, 16)
        sp.dma_start(wdec[RANK:2 * RANK, 256:512], w_decay[0, 1]).then_inc(dec_loaded, 16)

    steps = []
    for s in range(9):
        f = [8, 9, 0, 1, 2, 3, 4, 5, 6][s]
        b = [9, 8, 7, 6, 5, 4, 3, 2, 1][s]
        fs = [8, 0, 1, 2, 3, 4, 5, 6, 7]
        bs = [8, 7, 6, 5, 4, 3, 2, 1, 0]
        steps.append((0, f, None if s == 0 else fs[s - 1], fs[s]))
        steps.append((1, b, None if s == 0 else bs[s - 1], bs[s]))

    def gla_state_pe(pe, n_win_units):
        pe.wait_ge(win_evac, n_win_units)
        for ch in range(N_CHUNKS):
            if ch >= 2:
                pe.wait_ge(g_vcopy, ch - 1)
            for j in range(4):
                mm = pe.transpose(ps[4 + ch % 2][:, j * P:(j + 1) * P], gv_f[:, j, ch * P:(ch + 1) * P], ident)
            mm.then_inc(g_vt, 1)
        pe.wait_ge(dec_loaded, 32)
        for u, (j, c) in enumerate(dec_units):
            t0, w = ALL[c]
            if u >= 2:
                pe.wait_ge(g_min, u - 1)
            pe.matmul(ps[u % 2][:, 0:w], wdec[0:2 * RANK, j * P:(j + 1) * P], low_f[0:2 * RANK, t0:t0 + w],
                      start=True, stop=True).then_inc(g_logit, 1)
        for s, (d, ch, _, _) in enumerate(steps):
            if s >= 2:
                pe.wait_ge(g_kcopy, s - 1)
            pe.wait_ge(g_kk, 4)
            for t in range(2):
                mm = pe.transpose(ps[s % 2][:, t * P:(t + 1) * P], kk[:, 2 * d + t, ch * P:(ch + 1) * P], ident)
            mm.then_inc(g_kt, 1)
            pe.wait_ge(g_kcopy, s + 1)
            if s >= 2:
                pe.wait_ge(g_state, s - 1)
            pe.wait_ge(g_vcopy, N_CHUNKS)
            for hd in (0, 2, 1, 3):
                r = DK * (hd % 2)
                mm = pe.matmul(ps[2 + 2 * (s % 2) + hd % 2][r:r + DK, (hd // 2) * P:(hd // 2 + 1) * P],
                               ktok[:, s % 2, hd * DK:(hd + 1) * DK], vtok[:, ch, hd * DV:(hd + 1) * DV],
                               start=(hd < 2), stop=True, skip_group_check=True)
            mm.then_inc(g_ds, 1)

    def gla_state_act(act):
        for ch in range(N_CHUNKS):
            act.wait_ge(g_vt, ch + 1)
            nc.scalar.activation(vtok[:, ch, :], ps[4 + ch % 2][:, :], ACT.Copy).then_inc(g_vcopy, 1)
        for u, (j, c) in enumerate(dec_units):
            t0, w = ALL[c]
            b = cols_b[:, B_BDEC + j:B_BDEC + j + 1]
            act.wait_ge(g_logit, u + 1)
            if u >= 2:
                act.wait_ge(g_la, u - 1)
            nc.scalar.activation(lsa[:, u % 2, 0:w], ps[u % 2][:, 0:w], ACT.Abs, bias=b).then_inc(g_abs, 1)
            act.wait_ge(g_abs, u + 1)
            nc.scalar.activation(lsa[:, u % 2, 0:w], lsa[:, u % 2, 0:w], ACT.Exp, scale=-1.0).then_inc(g_exp, 1)
            act.wait_ge(g_exp, u + 1)
            nc.scalar.activation(lsa[:, u % 2, 0:w], lsa[:, u % 2, 0:w], ACT.Ln, bias=1.0).then_inc(g_ln, 1)
        act.wait_ge(g_last, 4)
        nc.scalar.activation(elast[:, :, :], last[:, :, :], ACT.Exp, scale=1.0 / GATE_NORM).then_inc(g_elast, 1)
        for j in range(4):
            act.wait_ge(g_diff, j + 1)
            nc.scalar.activation(dexp[:, j % 2, :], dexp[:, j % 2, :], ACT.Exp, scale=-1.0 / GATE_NORM)\
                .then_inc(g_dexp, 1)
        for s in range(len(steps)):
            act.wait_ge(g_kt, s + 1)
            if s >= 2:
                act.wait_ge(g_ds, s - 1)
            nc.scalar.activation(ktok[:, s % 2, :], ps[s % 2][:, 0:2 * P], ACT.Copy).then_inc(g_kcopy, 1)

    def gla_state_dve(dve):
        nc.vector.memset(wdec[0:2 * RANK, :], 0.0).then_inc(dec_zero, 1)
        for u, (j, c) in enumerate(dec_units):
            t0, w = ALL[c]
            b = cols_b[:, B_BDEC + j:B_BDEC + j + 1]
            dve.wait_ge(g_abs, u + 1)
            nc.vector.tensor_scalar(lsb[:, u % 2, 0:w], ps[u % 2][:, 0:w], b, 0.0, ALU.add, ALU.min)\
                .then_inc(g_min, 1)
            dve.wait_ge(g_min, u + 1)
            dve.wait_ge(g_ln, u + 1)
            nc.vector.tensor_tensor(la[:, j, t0:t0 + w], lsb[:, u % 2, 0:w], lsa[:, u % 2, 0:w], ALU.subtract)\
                .then_inc(g_la, 1)
        dve.wait_ge(g_la, len(dec_units))
        for j in range(4):
            for ch in range(N_CHUNKS):
                s = slice(ch * P, (ch + 1) * P)
                if j < 2:
                    o, i = cum[:, j, s], la[:, j, s]
                else:
                    o, i = cum[:, j, s][:, ::-1], la[:, j, s][:, ::-1]
                nc.vector.tensor_tensor_scan(o, ones, i, 0.0, ALU.mult, ALU.add).then_inc(g_scan, 1)
        dve.wait_ge(g_scan, 4 * N_CHUNKS)
        for j in range(4):
            v = cum[:, j, :].rearrange("p (n t) -> p n t", t=P)
            nc.vector.tensor_copy(last[:, j, :], v[:, :, P - 1] if j < 2 else v[:, :, 0]).then_inc(g_last, 1)
        dve.wait_ge(g_last, 4)

        def decayed_keys(j):
            dve.wait_ge(g_dexp, j + 1)
            nc.vector.tensor_tensor(kk[:, j, :], dexp[:, j % 2, :], gk_f[:, j % 2, :], ALU.mult).then_inc(g_kk, 1)
        for j in range(4):
            v = cum[:, j, :].rearrange("p (n t) -> p n t", t=P)
            if j >= 2:
                dve.wait_ge(g_kk, j - 1)
            nc.vector.tensor_tensor(dexp[:, j % 2, :].rearrange("p (n t) -> p n t", t=P), v,
                                    last[:, j, :].unsqueeze(2).to_broadcast([P, N_CHUNKS, P]),
                                    ALU.subtract).then_inc(g_diff, 1)
            if j >= 1:
                decayed_keys(j - 1)
        decayed_keys(3)
        dve.wait_ge(g_elast, 1)
        for s, (d, ch, src, dst) in enumerate(steps):
            dve.wait_ge(g_ds, s + 1)
            if s >= 2:
                dve.wait_ge(g_half, 2 * (s - 1))
            for t in range(2):
                for par in range(2):
                    r = slice(DK * par, DK * par + DK)
                    ds = ps[2 + 2 * (s % 2) + par][r, t * P:(t + 1) * P]
                    done = g_state if (t, par) == (1, 1) else g_half
                    if src is None:
                        nc.vector.tensor_copy(states[r, d, dst, t, :], ds).then_inc(done, 1)
                    else:
                        nc.vector.scalar_tensor_tensor(states[r, d, dst, t, :], states[r, d, src, t, :],
                                                       elast[r, 2 * d + t, ch:ch + 1], ds, ALU.mult, ALU.add)\
                            .then_inc(done, 1)

    g_half = sem("g_half")

    g_lq, g_eq, g_qk, g_sc, g_pred, g_oz, g_oc = (sem("g_lq"), sem("g_eq"), sem("g_qk"), sem("g_sc"), sem("g_pred"),
                                                  sem("g_oz"), sem("g_oc"))
    g_qd, g_qde = sem("g_qd"), sem("g_qde")
    N_SCORES = N_LEVELS + 1

    def bank_of(par, cc):
        return 2 * (cc // 2) + par

    def gla_intra_pe(pe):
        for hf in range(2):
            for lv in range(N_SCORES):
                g = hf * N_SCORES + lv
                pe.wait_ge(g_qk, 2 * g + 2)
                if lv > 0 or hf > 0:
                    pe.wait_ge(g_pred, 4 * g)
                if g == 0:
                    pe.wait_ge(g_state, len(steps))
                for cc in range(4):
                    for hd in range(GLA_HEADS):
                        r, t, par = slice(DK * (hd % 2), DK * (hd % 2) + DK), hd // 2, hd % 2
                        tok = slice(cc * P, (cc + 1) * P)
                        lat = slice(hf * 512 + cc * P, hf * 512 + (cc + 1) * P)
                        w = gk_f[r, t, lat] if lv == 0 else kc[r, t, tok]
                        col = ((cc % 2) * 2 + t) * P
                        mm = pe.matmul(ps[bank_of(par, cc)][:, col:col + P], w, qc[r, t, tok],
                                       start=True, stop=True)
                mm.then_inc(g_sc, 1)
            pe.wait_ge(g_pred, 4 * N_SCORES * (hf + 1))
            pe.wait_ge(g_qd, 2 * (hf + 1))
            if hf > 0:
                pe.wait_ge(g_oc, 4 * hf)
            for cc in range(4):
                ch = 4 * hf + cc
                for hd in range(GLA_HEADS):
                    r, t, par = slice(DK * (hd % 2), DK * (hd % 2) + DK), hd // 2, hd % 2
                    o = ps[4 + bank_of(par, cc)][:, ((cc % 2) * 2 + t) * P:((cc % 2) * 2 + t + 1) * P]
                    pe.matmul(o, vtok[:, ch, hd * DV:(hd + 1) * DV], scores[:, par, cc, t, :],
                              start=True, stop=False)
                    for d in range(2):
                        mm = pe.matmul(o, states[r, d, ch, t, :], qdec[r, d, t, cc * P:(cc + 1) * P],
                                       start=False, stop=(d == 1))
            mm.then_inc(g_oz, 1)

    def gla_intra_act(act):
        for hf in range(2):
            for d in range(2):
                if hf > 0:
                    act.wait_ge(g_oz, hf)
                tok = slice(hf * 512, (hf + 1) * 512)
                act.wait_ge(g_kt, len(steps))
                nc.scalar.activation(qdec[:, d, :, :], cum[:, 2 * d:2 * d + 2, tok], ACT.Exp,
                                     scale=1.0 / GATE_NORM).then_inc(g_qde, 1)
            for lv in range(1, N_SCORES):
                g = hf * N_LEVELS + lv - 1
                act.wait_ge(g_lq, 8 * g + 8)
                nc.scalar.activation(eq[:, :, :], eq[:, :, :], ACT.Exp, scale=1.0 / GATE_NORM).then_inc(g_eq, 1)
                nc.scalar.activation(ek[:, :, :], ek[:, :, :], ACT.Exp, scale=1.0 / GATE_NORM).then_inc(g_eq, 1)

    def gla_intra_dve(dve):
        dve.wait_ge(g_state, len(steps))
        for hf in range(2):
            tok = slice(hf * 512, (hf + 1) * 512)
            if hf > 0:
                dve.wait_ge(g_sc, hf * N_SCORES)
            nc.vector.tensor_scalar(qc[:, :, :], gq_f[:, :, tok], 2 * DK ** -0.5, None, ALU.mult).then_inc(g_qk, 2)
            for d in range(2):
                dve.wait_ge(g_qde, 2 * hf + d + 1)
                nc.vector.scalar_tensor_tensor(qdec[:, d, :, :], gq_f[:, :, tok], DK ** -0.5, qdec[:, d, :, :],
                                               ALU.mult, ALU.mult).then_inc(g_qd, 1)

            def differences(lv):
                g = hf * N_LEVELS + lv - 1
                if g > 0:
                    dve.wait_ge(g_qk, 2 * (hf * N_SCORES + lv))
                s = CHUNK >> lv
                for t in range(2):
                    def halves(a):
                        v = a.rearrange("p (n r s) -> p n r s", r=2, s=s)
                        return v[:, :, 0, :], v[:, :, 1, :]
                    fl, fr = halves(cum[:, t, tok])
                    bl, br = halves(cum[:, 2 + t, tok])
                    ql, qr = halves(eq[:, t, :])
                    kl_, kr_ = halves(ek[:, t, :])
                    n = 512 // (2 * s)
                    fref = fl[:, :, s - 1:s].to_broadcast([P, n, s])
                    bref = br[:, :, 0:1].to_broadcast([P, n, s])
                    nc.vector.tensor_tensor(qr, fr, fref, ALU.subtract).then_inc(g_lq, 1)
                    nc.vector.tensor_tensor(ql, bl, bref, ALU.subtract).then_inc(g_lq, 1)
                    nc.vector.tensor_tensor(kl_, fref, fl, ALU.subtract).then_inc(g_lq, 1)
                    nc.vector.tensor_tensor(kr_, bref, br, ALU.subtract).then_inc(g_lq, 1)

            def products(lv):
                g = hf * N_LEVELS + lv - 1
                dve.wait_ge(g_eq, 2 * g + 2)
                dve.wait_ge(g_sc, hf * N_SCORES + lv)
                nc.vector.scalar_tensor_tensor(qc[:, :, :], gq_f[:, :, tok], DK ** -0.5, eq[:, :, :],
                                               ALU.mult, ALU.mult).then_inc(g_qk, 1)
                nc.vector.tensor_tensor(kc[:, :, :], gk_f[:, :, tok], ek[:, :, :], ALU.mult).then_inc(g_qk, 1)

            def take(lv):
                g = hf * N_SCORES + lv
                dve.wait_ge(g_sc, g + 1)
                for b in range(4):
                    par, cp = b % 2, b // 2
                    dst = scores[:, par, 2 * cp:2 * cp + 2, :, :].rearrange("p c t i -> p (c t) i")
                    src = ps[b][:, :].rearrange("p (n i) -> p n i", i=P)
                    if lv == 0:
                        if hf > 0:
                            dve.wait_ge(g_oz, hf)
                        nc.vector.tensor_copy(dst, src).then_inc(g_pred, 1)
                    else:
                        dve.wait_ge(g_pred, 4 * g + b - 3)
                        m = cst[:, K_MASK + lv - 1:K_MASK + lv, :].bitcast(I32).to_broadcast([P, 4, P])
                        nc.vector.copy_predicated(dst, m, src).then_inc(g_pred, 1)
            differences(1)
            for lv in range(N_SCORES):
                if lv + 1 < N_SCORES:
                    products(lv + 1)
                    if lv + 2 < N_SCORES:
                        differences(lv + 2)
                take(lv)
            dve.wait_ge(g_oz, hf + 1)
            for cp in range(2):
                for par in range(2):
                    src = ps[4 + 2 * cp + par][:, :].rearrange("p (c t i) -> p t c i", c=2, t=2)
                    dst = gla_o[:, par::2, hf * 512 + cp * 256:hf * 512 + cp * 256 + 256]\
                        .rearrange("p t (c i) -> p t c i", c=2)
                    nc.vector.tensor_copy(dst, src).then_inc(g_oc, 1)

    z_loaded, o_sq, o_ss, o_ms, o_root, o_inv, o_norm, o_gate, o_hi, o_lo = (
        sem(n) for n in ("z_loaded", "o_sq", "o_ss", "o_ms", "o_root", "o_inv", "o_norm", "o_gate", "o_hi", "o_lo"))
    o_units = [(hd, c) for hd in range(GLA_HEADS) for c in range(2)]

    def gla_out_sp(sp):
        for n in range(4):
            sp.wait_ge(saved[n], 16 * 10)
        sp.wait_ge(g_oz, 2)
        sp.dma_start(gz_s[:, :, :], gate_dram[0:4].rearrange("n p t -> p n t")).then_inc(z_loaded, 16)

    def gla_out_act(act):
        def square(u):
            hd, c = o_units[u]
            if u == 0:
                act.wait_ge(g_oc, 8)
            if u >= 2:
                act.wait_ge(o_ss, u - 1)
            nc.scalar.activation(sq[:, u % 2, :], gla_o[:, hd, c * 512:(c + 1) * 512], ACT.Square).then_inc(o_sq, 1)
        square(0)
        for u in range(8):
            if u < 7:
                square(u + 1)
            act.wait_ge(o_ms, u + 1)
            nc.scalar.activation(eq[:, u % 2, :], eq[:, u % 2, :], ACT.Sqrt).then_inc(o_root, 1)

    def gla_out_pe(pe):
        for u in range(8):
            pe.wait_ge(o_sq, u + 1)
            if u >= 2:
                pe.wait_ge(o_ms, u - 1)
            pe.matmul(ps[u % 2][:, :], ones, sq[:, u % 2, :], start=True, stop=True).then_inc(o_ss, 1)

    def gla_out_dve(dve):
        def stat(u):
            dve.wait_ge(o_ss, u + 1)
            if u == 0:
                dve.wait_ge(g_qk, 4 * N_SCORES)
            nc.vector.tensor_scalar(eq[:, u % 2, :], ps[u % 2][:, :], 1.0 / DV, EPS, ALU.mult, ALU.add)\
                .then_inc(o_ms, 1)
        stat(0)
        dve.wait_ge(z_loaded, 16)
        for u, (hd, c) in enumerate(o_units):
            t = slice(c * 512, (c + 1) * 512)
            if u < 7:
                stat(u + 1) if u < 1 else None
            dve.wait_ge(o_root, u + 1)
            nc.vector.reciprocal(ek[:, u % 2, :], eq[:, u % 2, :]).then_inc(o_inv, 1)
            if 1 <= u < 7:
                stat(u + 1)
            dve.wait_ge(o_inv, u + 1)
            nc.vector.scalar_tensor_tensor(gla_n[:, 0, :], gla_o[:, hd, t], cols_b[:, B_GGLA:B_GGLA + 1],
                                           ek[:, u % 2, :], ALU.mult, ALU.mult).then_inc(o_norm, 1)
            dve.wait_ge(o_norm, u + 1)
            nc.vector.tensor_tensor(gla_n[:, 1, :], gla_n[:, 0, :], gz_s[:, hd, t], ALU.mult).then_inc(o_gate, 1)
            dve.wait_ge(o_gate, u + 1)
            nc.vector.tensor_copy(glah[:, hd, t], gla_n[:, 1, :]).then_inc(o_hi, 1)
            dve.wait_ge(o_hi, u + 1)
            nc.vector.tensor_tensor(glal[:, hd, t], gla_n[:, 1, :], glah[:, hd, t].bitcast(F32), ALU.subtract)\
                .then_inc(o_lo, 1)

    qk_units = [("k", 0, c) for c in range(3)] + [("q", t, c) for t in range(4) for c in range(2)]
    rope_loaded, k_sq, k_ss, k_ms, k_root, k_inv, k_norm, k_perm, k_a, k_b, k_rot, k_hi, k_lo = (
        sem(n) for n in ("rope_loaded", "k_sq", "k_ss", "k_ms", "k_root", "k_inv", "k_norm", "k_perm", "k_a", "k_b",
                         "k_rot", "k_hi", "k_lo"))
    v_turned, v_hi, v_lo = sem("v_turned"), sem("v_hi"), sem("v_lo")

    def qk_src(unit):
        kind, t, c = unit
        t0, w = ALL[c]
        return (k_f[:, t0:t0 + w] if kind == "k" else q_f[:, t, t0:t0 + w]), t0, w

    def qk_sp(sp):
        sp.wait_ge(o_lo, 8)
        sp.dma_start(rope_t[:, :, :], rope.rearrange("a p t -> p a t")).then_inc(rope_loaded, 16)

    def qk_act(act):
        act.wait_ge(o_lo, 8)
        def square(u):
            src, _, w = qk_src(qk_units[u])
            if u >= 2:
                act.wait_ge(k_ss, u - 1)
            nc.scalar.activation(qk_sq[:, u % 2, 0:w], src, ACT.Square).then_inc(k_sq, 1)
        square(0)
        for u in range(len(qk_units)):
            w = ALL[qk_units[u][2]][1]
            if u + 1 < len(qk_units):
                square(u + 1)
            act.wait_ge(k_ms, u + 1)
            nc.scalar.activation(qk_r[:, u % 2, 0:w], qk_r[:, u % 2, 0:w], ACT.Sqrt).then_inc(k_root, 1)

    def qk_pe(pe):
        pe.wait_ge(o_ms, 8)
        for n in range(3):
            for b in range(4 if n < 2 else 2):
                kt = 4 * n + b
                mm = pe.transpose(ps[4 + n][:, b * P:(b + 1) * P], v_f[:, kt * P:(kt + 1) * P], ident)
            mm.then_inc(v_turned, 1)

        def rotated(u):
            kind, t, c = qk_units[u]
            w = ALL[c][1]
            if c < 2:
                pe.wait_ge(k_norm, u + 1)
                if u >= 2:
                    pe.wait_ge(k_b, u - 1)
                pe.matmul(ps[2 + u % 2][:, 0:w], cst[:, K_PERM, :], qn[:, u % 2, 0:w], start=True, stop=True)\
                    .then_inc(k_perm, 1)
        for u in range(len(qk_units)):
            w = ALL[qk_units[u][2]][1]
            pe.wait_ge(k_sq, u + 1)
            if u >= 2:
                pe.wait_ge(k_ms, u - 1)
            pe.matmul(ps[u % 2][:, 0:w], cst[:, K_BLK, :], qk_sq[:, u % 2, 0:w], start=True, stop=True)\
                .then_inc(k_ss, 1)
            if u >= 1:
                rotated(u - 1)
        rotated(len(qk_units) - 1)

    def qk_dve(dve):
        for n in range(3):
            m = 4 if n < 2 else 2
            src = ps[4 + n][:, 0:m * P].rearrange("p (b g d) -> p b g d", b=m, g=2)
            dve.wait_ge(v_turned, n + 1)
            dve.wait_ge(g_oc, 8)
            nc.vector.tensor_copy(vv[:, 4 * n:4 * n + m, :, 0, :], src).then_inc(v_hi, 1)
            dve.wait_ge(v_hi, n + 1)
            nc.vector.tensor_tensor(vv[:, 4 * n:4 * n + m, :, 1, :], src,
                                    vv[:, 4 * n:4 * n + m, :, 0, :].bitcast(F32), ALU.subtract).then_inc(v_lo, 1)

        def stat(u):
            w = ALL[qk_units[u][2]][1]
            dve.wait_ge(k_ss, u + 1)
            nc.vector.tensor_scalar(qk_r[:, u % 2, 0:w], ps[u % 2][:, 0:w], 1.0 / HD, EPS, ALU.mult, ALU.add)\
                .then_inc(k_ms, 1)
        perms = 0
        hi_n = lo_n = 0
        dve.wait_ge(o_lo, 8)
        stat(0)
        dve.wait_ge(rope_loaded, 16)
        for u, unit in enumerate(qk_units):
            kind, t, c = unit
            src, t0, w = qk_src(unit)
            g = cols_b[:, (B_GK if kind == "k" else B_GQ):(B_GK if kind == "k" else B_GQ) + 1]
            dve.wait_ge(k_root, u + 1)
            nc.vector.reciprocal(qk_r[:, u % 2, 0:w], qk_r[:, u % 2, 0:w]).then_inc(k_inv, 1)
            if u + 1 < len(qk_units):
                stat(u + 1)
            dve.wait_ge(k_inv, u + 1)
            nc.vector.scalar_tensor_tensor(qn[:, u % 2, 0:w], src, g, qk_r[:, u % 2, 0:w], ALU.mult, ALU.mult)\
                .then_inc(k_norm, 1)
            dve.wait_ge(k_norm, u + 1)
            if c < 2:
                perms += 1
                nc.vector.tensor_tensor(rot[:, u % 2, 0:w], qn[:, u % 2, 0:w], rope_t[:, 0, t0:t0 + w], ALU.mult)\
                    .then_inc(k_a, 1)
                dve.wait_ge(k_perm, perms)
                nc.vector.tensor_tensor(rot_b[:, u % 2, 0:w], ps[2 + u % 2][:, 0:w], rope_t[:, 1, t0:t0 + w],
                                        ALU.mult).then_inc(k_b, 1)
                dve.wait_ge(k_a, perms)
                dve.wait_ge(k_b, u + 1)
                nc.vector.tensor_tensor(rot[:, u % 2, 0:w], rot[:, u % 2, 0:w], rot_b[:, u % 2, 0:w], ALU.add)\
                    .then_inc(k_rot, 1)
            else:
                nc.vector.tensor_copy(rot[:, u % 2, 0:w], qn[:, u % 2, 0:w]).then_inc(k_rot, 1)
                nc.vector.tensor_copy(rot_b[:, u % 2, 0:1], qn[:, u % 2, 0:1]).then_inc(k_b, 1)
            dve.wait_ge(k_rot, u + 1)
            for half in range(2):
                own = slice(HD * half, HD * half + HD)
                other = slice(HD * (1 - half), HD * (1 - half) + HD)
                r = rot[own, u % 2, 0:w]
                if kind == "q":
                    hd = 2 * t + half
                    nc.vector.tensor_copy(qs[own, hd, t0:t0 + w], r).then_inc(k_hi, 1)
                    hi_n += 1
                    dve.wait_ge(k_hi, hi_n)
                    nc.vector.tensor_tensor(qs[other, hd, t0:t0 + w], r, qs[own, hd, t0:t0 + w].bitcast(F32),
                                            ALU.subtract).then_inc(k_lo, 1)
                    lo_n += 1
                else:
                    nc.vector.tensor_copy(kh[own, half, t0:t0 + w], r).then_inc(k_hi, 1)
                    nc.vector.tensor_copy(kh[other, half, t0:t0 + w], r).then_inc(k_hi, 1)
                    hi_n += 2
                    dve.wait_ge(k_hi, hi_n)
                    for o in (own, other):
                        nc.vector.tensor_tensor(kl[o, half, t0:t0 + w], r, kh[own, half, t0:t0 + w].bitcast(F32),
                                                ALU.subtract).then_inc(k_lo, 1)
                    lo_n += 2

    N_K_LO = 3 * 4 + 8 * 2

    KCH = [(0, 512), (512, 512), (1024, 256)]
    s_done, mx_done, mt_done, nm_done, exp_done = (sem(n) for n in ("s_done", "mx_done", "mt_done", "nm_done", "exp_done"))
    t_done, p_hi, p_lo, pv_done = (sem(n) for n in ("t_done", "p_hi", "p_lo", "pv_done"))
    rt_done, ri_done, dg_done, rb_done, ot_done, os_done, of_done, a_hi, a_lo = (
        sem(n) for n in ("rt_done", "ri_done", "dg_done", "rb_done", "ot_done", "os_done", "of_done", "a_hi", "a_lo"))
    N_STEP = HEADS * 8
    TGROUPS = [(0, 4), (4, 8), (8, 10)]

    def att_where(i):
        u, qt = divmod(i, 4)
        hd, qb = divmod(u, 2)
        return u, hd, qb, qt

    def att_pe(pe):
        pe.wait_ge(k_lo, N_K_LO)
        pe.wait_ge(v_lo, 3)

        def score(i):
            u, hd, qb, qt = att_where(i)
            q0 = qb * 512 + qt * P
            for c, (t0, w) in enumerate(KCH):
                s = 3 * i + c
                if s >= 4:
                    pe.wait_ge(exp_done, s - 3)
                o = ps[s % 4][:, 0:w]
                kv = hd // (HEADS // KV_HEADS)
                pe.matmul(o, qs[:, hd, q0:q0 + P], kh[:, kv, t0:t0 + w], start=True, stop=False)
                pe.matmul(o, qs[:, hd, q0:q0 + P], kl[:, kv, t0:t0 + w], start=False, stop=True).then_inc(s_done, 1)

        def turn(i):
            pe.wait_ge(exp_done, 3 * i + 3)
            for r, (a, b) in enumerate(TGROUPS):
                n = 3 * i + r
                if n >= 2:
                    pe.wait_ge(p_lo, n - 1)
                for kt in range(a, b):
                    mm = pe.transpose(ps[4 + n % 2][:, (kt - a) * P:(kt - a + 1) * P],
                                      prob[:, i % 2, kt * P:(kt + 1) * P], ident)
                mm.then_inc(t_done, 1)

        def values(u):
            hd = u // 2
            kv = hd // (HEADS // KV_HEADS)
            pe.wait_ge(p_lo, 12 * (u + 1))
            if u >= 1:
                pe.wait_ge(os_done, u)
            for kt in range(TOK // P):
                w = vv[:, kt, kv, :, :].rearrange("p a d -> p (a d)")
                pe.matmul(ps[6][:, :], w, pth[:, kt, :], start=(kt == 0), stop=False)
                mm = pe.matmul(ps[6][:, :], w, ptl[:, kt, :], start=False, stop=(kt == TOK // P - 1))
            mm.then_inc(pv_done, 1)
            pe.wait_ge(dg_done, 4 * (u + 1))
            if u >= 1:
                pe.wait_ge(of_done, u)
            for qt in range(4):
                mm = pe.matmul(ps[7][:, qt * P:(qt + 1) * P], ones, diag[:, qt, :], start=True, stop=True)
            mm.then_inc(rb_done, 1)

        for i in range(N_STEP + 2):
            if i < N_STEP:
                score(i)
            if i >= 2 and (i - 2) % 4 == 3:
                values((i - 2) // 4)
            if 1 <= i <= N_STEP:
                turn(i - 1)

    def att_act(act):
        def exps(i):
            act.wait_ge(nm_done, i + 1)
            if i >= 2:
                act.wait_ge(t_done, 3 * (i - 1))
            for c, (t0, w) in enumerate(KCH):
                nc.scalar.activation(prob[:, i % 2, t0:t0 + w], ps[(3 * i + c) % 4][:, 0:w], ACT.Exp,
                                     bias=nmax[:, i:i + 1], scale=SCALE, accum_out=rs[:, i, c:c + 1])\
                    .then_inc(exp_done, 1)

        def high(i):
            u, hd, qb, qt = att_where(i)
            if qt == 0 and u >= 1:
                act.wait_ge(pv_done, u)
            for r, (a, b) in enumerate(TGROUPS):
                n = 3 * i + r
                act.wait_ge(t_done, n + 1)
                nc.scalar.activation(pth[:, a:b, qt * P:(qt + 1) * P],
                                     ps[4 + n % 2][:, 0:(b - a) * P].rearrange("p (k q) -> p k q", q=P),
                                     ACT.Copy).then_inc(p_hi, 1)

        def fold(u):
            act.wait_ge(pv_done, u + 1)
            if u >= 1:
                act.wait_ge(os_done, u)
            nc.scalar.activation(att_t[0:HD, 0, :], ps[6][HD:P, :], ACT.Copy).then_inc(ot_done, 1)
        for i in range(N_STEP + 2):
            if i < N_STEP:
                exps(i)
            if i >= 2 and (i - 2) % 4 == 3:
                fold((i - 2) // 4)
            if 1 <= i <= N_STEP:
                high(i - 1)

    def att_dve(dve):
        def maxima(i):
            for c, (t0, w) in enumerate(KCH):
                dve.wait_ge(s_done, 3 * i + c + 1)
                nc.vector.reduce_max(mx[:, i, c:c + 1], ps[(3 * i + c) % 4][:, 0:w], AX_X).then_inc(mx_done, 1)
            dve.wait_ge(mx_done, 3 * i + 3)
            nc.vector.reduce_max(mtot[:, i:i + 1], mx[:, i, 0:3], AX_X).then_inc(mt_done, 1)
            dve.wait_ge(mt_done, i + 1)
            nc.vector.tensor_scalar(nmax[:, i:i + 1], mtot[:, i:i + 1], -SCALE, None, ALU.mult).then_inc(nm_done, 1)

        def low(i):
            u, hd, qb, qt = att_where(i)
            for r, (a, b) in enumerate(TGROUPS):
                n = 3 * i + r
                dve.wait_ge(p_hi, n + 1)
                q = slice(qt * P, (qt + 1) * P)
                nc.vector.tensor_tensor(ptl[:, a:b, q],
                                        ps[4 + n % 2][:, 0:(b - a) * P].rearrange("p (k q) -> p k q", q=P),
                                        pth[:, a:b, q].bitcast(F32), ALU.subtract).then_inc(p_lo, 1)

        def inverse(i):
            qt = i % 4
            dve.wait_ge(exp_done, 3 * i + 3)
            nc.vector.reduce_sum(rtot[:, i:i + 1], rs[:, i, 0:3], AX_X).then_inc(rt_done, 1)
            dve.wait_ge(rt_done, i + 1)
            nc.vector.reciprocal(rinv[:, i:i + 1], rtot[:, i:i + 1]).then_inc(ri_done, 1)
            dve.wait_ge(ri_done, i + 1)
            if i >= 4:
                dve.wait_ge(rb_done, i // 4)
            nc.vector.tensor_scalar(diag[:, qt, :], ident, rinv[:, i:i + 1], None, ALU.mult).then_inc(dg_done, 1)

        def finish(u):
            hd, qb = divmod(u, 2)
            rows = slice(HD * (hd % 2), HD * (hd % 2) + HD)
            q = slice(qb * 512, (qb + 1) * 512)
            dve.wait_ge(ot_done, u + 1)
            nc.vector.tensor_tensor(att_t[0:HD, 1, :], ps[6][0:HD, :], att_t[0:HD, 0, :], ALU.add).then_inc(os_done, 1)
            dve.wait_ge(os_done, u + 1)
            dve.wait_ge(rb_done, u + 1)
            nc.vector.tensor_tensor(att_t[rows, 2, :], att_t[0:HD, 1, :], ps[7][0:HD, :], ALU.mult).then_inc(of_done, 1)
            dve.wait_ge(of_done, u + 1)
            nc.vector.tensor_copy(ah[rows, hd // 2, q], att_t[rows, 2, :]).then_inc(a_hi, 1)
            dve.wait_ge(a_hi, u + 1)
            nc.vector.tensor_tensor(al[rows, hd // 2, q], att_t[rows, 2, :], ah[rows, hd // 2, q].bitcast(F32),
                                    ALU.subtract).then_inc(a_lo, 1)
        for i in range(N_STEP + 2):
            if i < N_STEP:
                maxima(i)
            if i >= 2 and (i - 2) % 4 == 3:
                finish((i - 2) // 4)
            if 1 <= i <= N_STEP:
                inverse(i - 1)
                low(i - 1)

    gate_loaded = [sem("gate_loaded0"), sem("gate_loaded1")]
    m_done, m_t1, m_t2, m_sum, m_hi, m_lo = (sem(n) for n in ("m_done", "m_t1", "m_t2", "m_sum", "m_hi", "m_lo"))
    w_done, w_res = sem("w_done"), sem("w_res")
    h_back = sem("h_back")

    def merge_sp(sp, panel0):
        wb = w_branch[0].rearrange("b (k p) n -> p (b k) n", p=P)
        sp.wait_ge(a_lo, 2 * HEADS)
        for n in range(KT):
            load_panel(sp, pn(panel0 + n), raw[:, (panel0 + n) % 2, :].rearrange("p (k n) -> p k n", k=KT),
                       wb[:, :, n * P:(n + 1) * P])
            if n >= 2:
                sp.wait_ge(m_t2, 2 * (n - 1))
            sp.dma_start(merge_gate[:, n % 2, :, :],
                         gate_dram[4:20].rearrange("(b n) p t -> p b n t", b=2)[:, :, n, :])\
                .then_inc(gate_loaded[n % 2], 16)
        wo = w_out[0].rearrange("(k p) n -> p k n", p=P)
        for n in range(KT):
            load_panel(sp, pn(panel0 + KT + n), raw[:, (panel0 + KT + n) % 2, :].rearrange("p (k n) -> p k n", k=KT),
                       wo[:, :, n * P:(n + 1) * P])
            if n == 0:
                sp.wait_ge(panel_used, panel0 + KT)
                sp.wait_ge(h_saved, 16)
                sp.dma_start(h1[:, :, :], h_dram).then_inc(h_back, 16)

    def merge_pe(pe, panel0):
        pe.wait_ge(a_lo, 16)
        for n in range(KT):
            p = panel0 + n
            wait_panel(pe, pn(p))
            for b, (hi, lo) in enumerate(((ah, al), (glah, glal))):
                for c, (t0, w) in enumerate(LAT):
                    u = 4 * n + 2 * b + c
                    if u >= 8:
                        pe.wait_ge(m_t2 if b else m_t1, 2 * (n - 2) + c + 1)
                    for k in range(4):
                        cols = slice((4 * b + k) * P, (4 * b + k + 1) * P)
                        mm = three(pe, ps[u % 8][:, :], wh[:, p % 2, cols], wl[:, p % 2, cols],
                                   hi[:, k, t0:t0 + w], lo[:, k, t0:t0 + w], k == 0, k == 3)
                    mm.then_inc(m_done if (b, c) != (1, 1) else panel_used, 1)
        pe.wait_ge(m_lo, 16)
        for n in range(KT):
            p = panel0 + KT + n
            wait_panel(pe, pn(p))
            for c, (t0, w) in enumerate(LAT):
                u = 2 * n + c
                if u >= 8:
                    pe.wait_ge(w_res, u - 7)
                for k in range(KT):
                    cols = slice(k * P, (k + 1) * P)
                    mm = three(pe, ps[u % 8][:, :], wh[:, p % 2, cols], wl[:, p % 2, cols],
                               mh[:, k, t0:t0 + w], ml[:, k, t0:t0 + w], k == 0, k == KT - 1)
                mm.then_inc(w_done if c == 0 else panel_used, 1)

    def merge_dve(dve, panel0):
        split_panel(dve, pn(panel0))
        for n in range(KT):
            p = panel0 + n
            split_panel(dve, pn(p + 1))
            dve.wait_ge(gate_loaded[n % 2], 16 * (n // 2 + 1))
            for b in range(2):
                for c, (t0, w) in enumerate(LAT):
                    if (b, c) == (1, 1):
                        dve.wait_ge(panel_used, p + 1)
                    else:
                        dve.wait_ge(m_done, 3 * n + 2 * b + c + 1)
                    nc.vector.tensor_tensor((mb if b else ma)[:, c, :], ps[(4 * n + 2 * b + c) % 8][:, :],
                                            merge_gate[:, n % 2, b, t0:t0 + w], ALU.mult)\
                        .then_inc(m_t2 if b else m_t1, 1)
            for c, (t0, w) in enumerate(LAT):
                u = 2 * n + c
                dve.wait_ge(m_t2, u + 1)
                dve.wait_ge(m_t1, u + 1)
                nc.vector.tensor_tensor(ma[:, c, :], ma[:, c, :], mb[:, c, :], ALU.add).then_inc(m_sum, 1)
                dve.wait_ge(m_sum, u + 1)
                nc.vector.tensor_copy(mh[:, n, t0:t0 + w], ma[:, c, :]).then_inc(m_hi, 1)
                dve.wait_ge(m_hi, u + 1)
                nc.vector.tensor_tensor(ml[:, n, t0:t0 + w], ma[:, c, :], mh[:, n, t0:t0 + w].bitcast(F32),
                                        ALU.subtract).then_inc(m_lo, 1)
        for n in range(KT):
            p = panel0 + KT + n
            if n + 1 < KT:
                split_panel(dve, pn(p + 1))
            if n == 0:
                dve.wait_ge(h_back, 16)
            for c, (t0, w) in enumerate(LAT):
                if c == 0:
                    dve.wait_ge(w_done, n + 1)
                else:
                    dve.wait_ge(panel_used, p + 1)
                hk = h1[:, n, t0:t0 + w]
                nc.vector.scalar_tensor_tensor(hk, ps[(2 * n + c) % 8][:, :], gates[:, 1, n, 0:1], hk,
                                               ALU.mult, ALU.add).then_inc(w_res, 1)

    norm0 = Norm(0, 0, h0, nh0, nl0, ALL)
    ffn0 = Ffn("f0", 0, 0, h0, norm0, hidh0, hidl0, ALL, PANEL0)
    norm1 = Norm(3, 1, h0, nh0, nl0, ALL)
    win_p0 = ffn0.end_panel
    merge_p0 = win_p0 + len(win)
    norm2 = Norm(6, 2, h1, n1h, n1l, LAT)
    ffn1_p0 = merge_p0 + 2 * KT
    ffn1 = Ffn("f1", 1, 2, h1, norm2, hidh1, hidl1, LAT, ffn1_p0)
    norm3 = Norm(8, 0, h1, None, None, LAT, final=y_fin)

    def once(f):
        return lambda eng, c, k: f(eng) if (c, k) == (0, 0) else None

    block = stack.enter_context(nc.Block())

    @block.sync
    def _(sp):
        load_sp(sp)
        ffn0.sp(sp)
        win_sp(sp, win_p0, ffn0, norm1)
        gla_setup_sp(sp)
        gla_out_sp(sp)
        qk_sp(sp)
        merge_sp(sp, merge_p0)
        ffn1.sp(sp)
        result_sp(sp)

    @block.scalar
    def _(act):
        load_act(act)

        def ready0(act):
            act.wait_ge(turn_evac_v, 10)
            act.wait_ge(turn_evac_s, 10)
            act.wait_ge(coef_done, 6)
        norm0.act(act, once(ready0))
        ffn0.act(act)
        norm1.act(act, once(ffn0.wait_end))
        win_act(act, win_p0)
        gla_state_act(act)
        gla_intra_act(act)
        gla_out_act(act)
        qk_act(act)
        att_act(act)
        norm2.act(act, once(lambda a: a.wait_ge(w_res, 16)))
        ffn1.act(act)
        norm3.act(act, once(ffn1.wait_end))
        result_copy(act, 1, lambda o, i: nc.scalar.activation(o, i, ACT.Copy), fin_evac_s)

    @block.tensor
    def _(pe):
        pe.sem_inc(panel_used, PANEL0)
        load_pe(pe)
        norm0.pe(pe)
        ffn0.pe(pe)
        norm1.pe(pe)
        win_pe(pe, win_p0, norm1)
        gla_state_pe(pe, len(win_units))
        gla_intra_pe(pe)
        gla_out_pe(pe)
        qk_pe(pe)
        att_pe(pe)
        merge_pe(pe, merge_p0)
        norm2.pe(pe)
        ffn1.pe(pe)
        norm3.pe(pe)
        result_pe(pe, lambda pe, i: pe.wait_ge(norm3.scaled, norm3.u0 + KT * (1 + i // 4)) if i % 4 == 0 else None)

    @block.vector
    def _(dve):
        dve.sem_inc(panel_split, 2 * PANEL0)
        load_dve(dve)
        dve.wait_ge(turn_evac_s, 10)
        norm0.dve(dve)
        ffn0.dve(dve)
        ffn0.wait_end(dve)
        norm1.dve(dve)
        win_dve(dve, win_p0)
        dve.wait_ge(win_evac, len(win_units))
        gla_state_dve(dve)
        gla_intra_dve(dve)
        gla_out_dve(dve)
        qk_dve(dve)
        att_dve(dve)
        merge_dve(dve, merge_p0)
        dve.wait_ge(w_res, 16)
        norm2.dve(dve)
        ffn1.dve(dve)
        ffn1.wait_end(dve)
        norm3.dve(dve)
        result_copy(dve, 0, lambda o, i: nc.vector.tensor_copy(o, i), fin_evac_v)

    stack.close()


_INS = ["x", "c", "ctx", "c_ctx", "w_mod", "b_mod", "g_norm", "w_ffn_up", "w_ffn_down", "w_in", "g_q", "g_k",
        "w_decay", "b_decay", "g_gla", "w_branch", "b_gate", "w_out", "g_final"]
_OUTS = [((1, SEQ, D), "float32")]


def kernel(**inputs):
    import numpy as _np
    import concourse.bacc as _bacc
    from concourse import mybir as _mybir
    from concourse.bass_utils import run_bass_kernel_spmd as _run

    nc = _bacc.Bacc("TRN2", target_bir_lowering=False, num_devices=1)
    arrays, args = {}, []
    given = {name: _np.ascontiguousarray(inputs[name]) for name in _INS}
    given["shape_consts"] = shape_constants()
    given["rope_tables"] = rope_tables()
    for name, a in given.items():
        arrays[f"in_{name}_dram"] = a
        args.append(nc.dram_tensor(f"in_{name}_dram", a.shape, _mybir.dt.from_np(a.dtype), kind="ExternalInput").ap())
    for i, (shape, dtype) in enumerate(_OUTS):
        dt = _mybir.dt.from_np(_np.dtype(dtype))
        args.append(nc.dram_tensor(f"out_{i}_dram", shape, dt, kind="ExternalOutput").ap())
    build(nc, *args)
    r = _run(nc, [arrays], core_ids=[0])
    got = tuple(r.results[0][f"out_{i}_dram"] for i in range(len(_OUTS)))
    return got[0]
```

```python
from contextlib import ExitStack

import concourse.bass as bass
from concourse import mybir
import numpy as np

F32 = mybir.dt.float32
F32R = mybir.dt.float32r
I32 = mybir.dt.int32
ALU = mybir.AluOpType
ACT = mybir.ActivationFunctionType
AX_X = mybir.AxisListType.X

P = 128
D = 1024
KT = D // P
SEQ = 1024
CTX = 256
TOK = SEQ + CTX
D_FF = 2816
EPS = 1e-6
HEADS, KV_HEADS, HD = 8, 2, 64
GLA_HEADS, DK, DV = 4, 64, 128
RANK = 16
GATE_NORM = 16.0
GRID_W = 64
ROPE_THETA = 10000.0
SCALE = HD ** -0.5

LAT = [(0, 512), (512, 512)]
ALL = LAT + [(1024, 256)]

C_Q, C_K, C_V = 0, 512, 640
C_GQ, C_GK, C_GV, C_GZ, C_LOW, C_GATE = 768, 1024, 1280, 1792, 2304, 2336

A_BMOD, A_GNORM, A_GFINAL, A_BGATE, A_C = 0, 72, 96, 104, 120
B_CCTX, B_BDEC, B_GGLA, B_GQ, B_GK = 0, 8, 12, 13, 14
B_ROWS = 15

N_LEVELS = 7
K_ID, K_ONES, K_BLK, K_PERM, K_MASK = 0, 1, 2, 3, 4
N_CONST = K_MASK + N_LEVELS

PANEL0 = 2
CHUNK = 128
N_CHUNKS = TOK // CHUNK
LAT_CHUNKS = SEQ // CHUNK



def shape_constants():
    c = np.zeros((P, N_CONST, P), np.float32)
    i = np.arange(P)
    c[i, K_ID, i] = 1
    c[:, K_ONES] = 1
    c[:, K_BLK] = (i[:, None] // HD == i[None, :] // HD)
    c[i, K_PERM, i ^ (HD // 2)] = 1
    for n in range(N_LEVELS):
        half = CHUNK >> (n + 1)
        same = i[:, None] // (2 * half) == i[None, :] // (2 * half)
        other = (i[:, None] // half) != (i[None, :] // half)
        c[:, K_MASK + n] = same & other
    return c.reshape(P, N_CONST * P)


def rope_tables():
    axis = HD // 2
    freqs = np.float32(ROPE_THETA) ** (-np.arange(0, axis, 2, dtype=np.float32) / np.float32(axis))
    t = np.arange(SEQ)
    row, col = (t // GRID_W).astype(np.float32), (t % GRID_W).astype(np.float32)
    ang = np.concatenate([row[:, None] * freqs, col[:, None] * freqs], axis=-1).astype(np.float32)
    d = np.arange(P)
    sign = np.where(d % HD < HD // 2, -1, 1).astype(np.float32)
    cos, sin = np.cos(ang).T, np.sin(ang).T
    return np.stack([cos[d % axis], sin[d % axis] * sign[:, None]]).astype(np.float32)


def build(nc, x, c, ctx_in, c_ctx, w_mod, b_mod, g_norm, w_ffn_up, w_ffn_down, w_in, g_q, g_k,
          w_decay, b_decay, g_gla, w_branch, b_gate, w_out, g_final, consts, rope, out):
    stack = ExitStack()
    base = 16512

    def at(name, kb, shape, dt=F32):
        return nc.alloc_sbuf_tensor_at(name, [P, *shape], dt, offset=base + int(kb * 1024))

    def sem(name):
        return stack.enter_context(nc.semaphore(name))

    h0 = at("h0", 0, [KT, TOK])
    nh0, nl0 = at("nh0", 40, [KT, TOK], F32R), at("nl0", 80, [KT, TOK], F32R)
    x_rows = at("x_rows", 40, [TOK // P, D])
    mod_raw = [at("mod_raw0", 120, [4, 512]), at("mod_raw1", 128, [4, 512]), at("mod_raw2", 164, [4, 512])]
    mod_raw_late = [at("mod_raw_late0", 140, [4, 512]), at("mod_raw_late1", 172, [4, 512]),
                    at("mod_raw_late2", 164, [4, 512])]
    mod_row = at("mod_row", 201, [2, 512])
    hidh0, hidl0 = at("hidh0", 120, [2, TOK], F32R), at("hidl0", 130, [2, TOK], F32R)
    raw = at("raw", 140, [2, 1024])
    wh, wl = at("wh", 148, [2, 1024], F32R), at("wl", 156, [2, 1024], F32R)
    silu_a = at("silu_a", 164, [3, 512])
    prod = at("prod", 170, [2, 512])
    sq = at("sq", 174, [2, 512])
    rstd = at("rstd", 178, [TOK])
    cols_a, cols_b = at("cols_a", 183, [P]), at("cols_b", 183.5, [16])
    modv = at("modv", 184, [72, 2])
    coef = at("coef", 184.75, [3, KT, 2])
    gates = at("gates", 185, [3, KT, 2])
    silu_c = at("silu_c", 185.25, [KT, 2])
    cst = at("cst", 185.5, [N_CONST, P])
    vec_a, vec_b = at("vec_a", 193, [P]), at("vec_b", 193.5, [P])
    norm_t = at("norm_t", 193, [2, 512])
    sq_sum = at("sq_sum", 197, [2, 512])
    y_rows = at("y_rows", 72, [SEQ // P, D])
    h1 = at("h1", 40, [KT, SEQ])
    n1h, n1l = at("n1h", 0, [KT, SEQ], F32R), at("n1l", 72, [KT, SEQ], F32R)
    hidh1, hidl1 = at("hidh1", 120, [2, SEQ], F32R), at("hidl1", 128, [2, SEQ], F32R)
    y_fin = at("y_fin", 0, [KT, SEQ])

    eps = cols_b[:, B_ROWS:B_ROWS + 1]
    ident = cst[:, K_ID, :]
    ones = cst[:, K_ONES, :]

    psum = stack.enter_context(nc.psum_tensor("psum", [P, 8 * 512], F32))
    ps = [psum[:, 512 * i:512 * (i + 1)] for i in range(8)]

    raw_loaded = [sem("raw_loaded0"), sem("raw_loaded1")]
    panel_split = sem("panel_split")
    panel_used = sem("panel_used")
    vec_loaded = sem("vec_loaded")
    const_loaded = sem("const_loaded")
    rows_loaded = [sem(f"rows_loaded{i}") for i in range(TOK // P)]
    cols_ready = sem("cols_ready")
    cols_copied = sem("cols_copied")
    turned = sem("turned")
    turn_evac_v, turn_evac_s = sem("turn_evac_v"), sem("turn_evac_s")
    silu_c_done = sem("silu_c_done")
    mod_loaded = [sem(f"mod_loaded{i}") for i in range(3)]
    mod_product = sem("mod_product")
    mod_copied, mod_turned = sem("mod_copied"), sem("mod_turned")
    mod_evac = sem("mod_evac")
    coef_done = sem("coef_done")
    out_stored = [sem("out_stored0"), sem("out_stored1")]
    fin_turned, fin_evac_v, fin_evac_s = sem("fin_turned"), sem("fin_evac_v"), sem("fin_evac_s")

    def split_panel(dve, p, n=1024):
        q, par = p
        dve.wait_ge(raw_loaded[par], 16 * q)
        dve.wait_ge(panel_used, 2 * q + par - 1)
        nc.vector.tensor_copy(wh[:, par, 0:n], raw[:, par, 0:n]).then_inc(panel_split, 1)
        dve.wait_ge(panel_split, 4 * q + 2 * par + 1)
        nc.vector.tensor_tensor(wl[:, par, 0:n], raw[:, par, 0:n], wh[:, par, 0:n].bitcast(F32),
                                ALU.subtract).then_inc(panel_split, 1)

    def pn(p):
        return (p // 2, p % 2)

    def load_panel(sp, p, dst, src):
        q, par = p
        sp.wait_ge(panel_split, 4 * q + 2 * par - 2)
        sp.dma_start(dst, src).then_inc(raw_loaded[par], 16)

    def wait_panel(pe, p):
        q, par = p
        pe.wait_ge(panel_split, 4 * q + 2 * par + 2)

    def three(pe, o, hi_w, lo_w, hi_x, lo_x, first, last):
        pe.matmul(o, hi_w, hi_x, start=first, stop=False)
        pe.matmul(o, hi_w, lo_x, start=False, stop=False)
        return pe.matmul(o, lo_w, hi_x, start=False, stop=last)

    MOD_BLOCKS = 9 * D // 512
    MOD_GROUP = MOD_BLOCKS // 3

    MOD_LATE = 4 * MOD_GROUP

    def mod_slot(p):
        return (mod_raw if p < MOD_LATE else mod_raw_late)[p % 3]

    def mod_load(sp, p):
        n, half = p // 2, p % 2
        if p >= 3:
            sp.wait_ge(mod_product, p - 2)
        src = w_mod[0].rearrange("(k p) n -> p k n", p=P)[:, 4 * half:4 * half + 4, n * 512:(n + 1) * 512]
        sp.dma_start(mod_slot(p)[:, :, :], src).then_inc(mod_loaded[p % 3], 16)

    def load_sp(sp):
        rows = lambda a: a.rearrange("(r c) -> r c", c=P)
        vec = [
            (vec_a[A_BMOD:A_BMOD + 72, :], rows(b_mod[0])),
            (vec_a[A_GNORM:A_GNORM + 24, :], g_norm[0].rearrange("i (r c) -> (i r) c", c=P)),
            (vec_a[A_GFINAL:A_GFINAL + 8, :], rows(g_final)),
            (vec_a[A_BGATE:A_BGATE + 16, :], rows(b_gate[0])),
            (vec_a[A_C:A_C + 8, :], rows(c[0])),
            (vec_b[B_CCTX:B_CCTX + 8, :], rows(c_ctx)),
            (vec_b[B_BDEC:B_BDEC + 4, :], b_decay[0].rearrange("i (r c) -> (i r) c", c=P)),
            (vec_b[B_GGLA:B_GGLA + 1, :], g_gla),
            (vec_b[B_GQ:B_GQ + 1, 0:HD], g_q), (vec_b[B_GQ:B_GQ + 1, HD:P], g_q),
            (vec_b[B_GK:B_GK + 1, 0:HD], g_k), (vec_b[B_GK:B_GK + 1, HD:P], g_k),
        ]
        sp.dma_start(cst[:, :, :], consts.rearrange("p (n c) -> p n c", c=P)).then_inc(const_loaded, 16)
        for dst, src in vec:
            sp.dma_start(dst, src).then_inc(vec_loaded, 16)
        for i in range(TOK // P):
            src = x[0, i * P:(i + 1) * P, :] if i < SEQ // P else ctx_in[0, i * P - SEQ:(i + 1) * P - SEQ, :]
            sp.dma_start(x_rows[:, i, :], src).then_inc(rows_loaded[i], 16)
        for p in range(MOD_LATE):
            mod_load(sp, p)

    N_VEC_DMA = 12

    def load_pe(pe):
        pe.wait_ge(const_loaded, 16)
        pe.wait_ge(vec_loaded, 16 * N_VEC_DMA)
        pe.transpose(ps[7][:, 0:P], vec_a[:, :], ident).then_inc(cols_ready, 1)
        pe.transpose(ps[7][:, P:P + B_ROWS], vec_b[0:B_ROWS, :], ident[0:B_ROWS, 0:B_ROWS]).then_inc(cols_ready, 1)
        for i in range(TOK // P):
            pe.wait_ge(rows_loaded[i], 16)
            for q in range(2):
                u = 2 * i + q
                if u >= 6:
                    pe.wait_ge(turn_evac_s if q else turn_evac_v, (u - 6) // 2 + 1)
                for k in range(4):
                    mm = pe.transpose(ps[u % 6][:, k * P:(k + 1) * P],
                                      x_rows[:, i, (4 * q + k) * P:(4 * q + k + 1) * P], ident)
                mm.then_inc(turned, 1)
        pe.wait_ge(silu_c_done, 2)
        pe.wait_ge(cols_copied, 3)
        pe.wait_ge(turn_evac_v, 10)
        pe.wait_ge(turn_evac_s, 10)

    def mod_pe(pe, blocks, to_turn):
        def turn(n):
            pe.wait_ge(mod_copied, n + 1)
            for q in range(4):
                m = 4 * (n % MOD_GROUP) + q
                mm = pe.transpose(ps[3 + n // MOD_GROUP][:, 2 * m:2 * m + 2],
                                  mod_row[0:2, n % 2, q * P:(q + 1) * P], ident[0:2, 0:2])
            mm.then_inc(mod_turned, 1)
        for n in blocks:
            if n >= 2:
                pe.wait_ge(mod_copied, n - 1)
            for half in range(2):
                p = 2 * n + half
                pe.wait_ge(mod_loaded[p % 3], 16 * (p // 3 + 1))
                for k in range(4):
                    mm = pe.matmul(ps[6 + n % 2][0:2, :], silu_c[:, 4 * half + k, :], mod_slot(p)[:, k, :],
                                   start=(p % 2 == 0 and k == 0), stop=(p % 2 == 1 and k == 3))
                mm.then_inc(mod_product, 1)
            if n - 2 in to_turn:
                turn(n - 2)
        for n in (blocks[-1] - 1, blocks[-1]):
            if n in to_turn:
                turn(n)

    def mod_copy(dve, n):
        dve.wait_ge(mod_product, 2 * (n + 1))
        if n >= 2:
            dve.wait_ge(mod_turned, n - 1)
        nc.vector.tensor_copy(mod_row[0:2, n % 2, :], ps[6 + n % 2][0:2, :]).then_inc(mod_copied, 1)

    def mod_finish(dve, i):
        dve.wait_ge(mod_turned, MOD_GROUP * (i + 1))
        nc.vector.tensor_tensor(modv[:, 24 * i:24 * i + 24, :],
                                ps[3 + i][:, 0:48].rearrange("p (n s) -> p n s", s=2),
                                cols_a[:, A_BMOD + 24 * i:A_BMOD + 24 * i + 24].unsqueeze(2)
                                .to_broadcast([P, 24, 2]), ALU.add).then_inc(mod_evac, 1)
        dve.wait_ge(mod_evac, i + 1)
        nc.vector.scalar_tensor_tensor(
            coef[:, i, :, :], modv[:, 8 * (3 * i + 1):8 * (3 * i + 2), :], 1.0,
            cols_a[:, A_GNORM + 8 * i:A_GNORM + 8 * i + 8].unsqueeze(2).to_broadcast([P, 8, 2]),
            ALU.add, ALU.mult).then_inc(coef_done, 1)
        nc.vector.tensor_scalar(gates[:, i, :, :], modv[:, 8 * (3 * i + 2):8 * (3 * i + 3), :],
                                1.0 if i == 1 else 0.5, None, ALU.mult).then_inc(coef_done, 1)

    def turn_evac(nc_copy, q, done):
        for i in range(TOK // P):
            u = 2 * i + q
            nc_copy(u, h0[:, 4 * q:4 * q + 4, i * P:(i + 1) * P],
                    ps[u % 6][:, :].rearrange("p (k t) -> p k t", k=4)).then_inc(done, 1)

    def load_act(act):
        act.wait_ge(cols_copied, 3)
        nc.scalar.activation(silu_c[:, :, 0], cols_a[:, A_C:A_C + 8], ACT.Silu).then_inc(silu_c_done, 1)
        nc.scalar.activation(silu_c[:, :, 1], cols_b[:, B_CCTX:B_CCTX + 8], ACT.Silu).then_inc(silu_c_done, 1)

        def copy(u, o, i):
            act.wait_ge(turned, u + 1)
            return nc.scalar.activation(o, i, ACT.Copy)
        turn_evac(copy, 1, turn_evac_s)

    def load_dve(dve):
        nc.vector.memset(eps, EPS).then_inc(cols_copied, 1)
        dve.wait_ge(cols_ready, 2)
        nc.vector.tensor_copy(cols_a[:, :], ps[7][:, 0:P]).then_inc(cols_copied, 1)
        nc.vector.tensor_copy(cols_b[:, 0:B_ROWS], ps[7][:, P:P + B_ROWS]).then_inc(cols_copied, 1)

        def copy(u, o, i):
            dve.wait_ge(turned, u + 1)
            return nc.vector.tensor_copy(o, i)
        turn_evac(copy, 0, turn_evac_v)
        dve.wait_ge(cols_copied, 3)

    class Norm:
        sq_done, sq_used = sem("sq_done"), sem("sq_used")
        root_done, rstd_done = sem("root_done"), sem("rstd_done")
        scaled, hi_done, lo_done = sem("scaled"), sem("hi_done"), sem("lo_done")
        total_done = sem("total_done")

        def __init__(self, c0, i, h, hi, lo, chunks, final=None):
            self.i, self.h, self.hi, self.lo, self.chunks, self.final = i, h, hi, lo, chunks, final
            self.c0, self.u0 = c0, KT * c0

        def normed(self, eng, c):
            eng.wait_ge(self.lo_done, self.u0 + KT * (c + 1))

        def act(self, act, ready, early=False):
            C = len(self.chunks)

            def square(c, k):
                t0, w = self.chunks[c]
                u = c * KT + k
                ready(act, c, k)
                if u >= 2:
                    act.wait_ge(self.sq_used, self.u0 + u - 1)
                nc.scalar.activation(sq[:, u % 2, 0:w], self.h[:, k, t0:t0 + w], ACT.Square)\
                    .then_inc(self.sq_done, 1)

            def root(c):
                t0, w = self.chunks[c]
                if early:
                    act.wait_ge(self.total_done, c + 1)
                else:
                    act.wait_ge(self.sq_used, self.u0 + KT * (c + 1))
                nc.scalar.activation(rstd[:, t0:t0 + w], ps[c][:, 0:w], ACT.Sqrt, bias=eps, scale=1.0 / D)\
                    .then_inc(self.root_done, 1)

            def high(c, k):
                t0, w = self.chunks[c]
                s = 1 if t0 >= SEQ else 0
                u = c * KT + k
                act.wait_ge(self.scaled, self.u0 + u + 1)
                nc.scalar.activation(self.hi[:, k, t0:t0 + w], norm_t[:, u % 2, 0:w], ACT.Identity,
                                     bias=modv[:, 8 * 3 * self.i + k, s:s + 1]).then_inc(self.hi_done, 1)

            if early:
                for c in range(C):
                    for k in range(KT):
                        square(c, k)
                    root(c)
            else:
                for k in range(KT):
                    square(0, k)
            for c in range(C):
                if not early:
                    root(c)
                for k in range(KT):
                    if self.final is None:
                        high(c, k)
                    if c + 1 < C and not early:
                        square(c + 1, k)

        def pe(self, pe):
            for c, (t0, w) in enumerate(self.chunks):
                for k in range(KT):
                    u = c * KT + k
                    pe.wait_ge(self.sq_done, self.u0 + u + 1)
                    pe.matmul(ps[c][:, 0:w], ones, sq[:, u % 2, 0:w], start=(k == 0), stop=(k == KT - 1))\
                        .then_inc(self.sq_used, 1)

        def early_sums(self, dve, after):
            for c, (t0, w) in enumerate(self.chunks):
                acc = sq_sum[:, c % 2, 0:w]
                for k in range(KT):
                    u = c * KT + k
                    dve.wait_ge(self.sq_done, u + 1)
                    if k == 0:
                        if c >= 2:
                            dve.wait_ge(self.total_done, c - 1)
                        nc.vector.tensor_copy(acc, sq[:, u % 2, 0:w]).then_inc(self.sq_used, 1)
                    else:
                        dve.wait_ge(self.sq_used, u)
                        nc.vector.tensor_tensor(acc, acc, sq[:, u % 2, 0:w], ALU.add).then_inc(self.sq_used, 1)
                after(c)

        def early_pe(self, pe, after):
            for c, (t0, w) in enumerate(self.chunks):
                pe.wait_ge(self.sq_used, KT * (c + 1))
                pe.matmul(ps[c][:, 0:w], ones, sq_sum[:, c % 2, 0:w], start=True, stop=True)\
                    .then_inc(self.total_done, 1)
                after(c)

        def inverse(self, dve, c):
            t0, w = self.chunks[c]
            dve.wait_ge(self.root_done, self.c0 + c + 1)
            nc.vector.reciprocal(rstd[:, t0:t0 + w], rstd[:, t0:t0 + w]).then_inc(self.rstd_done, 1)

        def dve(self, dve, after=lambda u: None, early=False):
            n = len(self.chunks)
            if self.final is None:
                dve.wait_ge(coef_done, 2 * (self.i + 1))

            def lo(u):
                c, k = divmod(u, KT)
                t0, w = self.chunks[c]
                s = 1 if t0 >= SEQ else 0
                dve.wait_ge(self.hi_done, self.u0 + u + 1)
                nc.vector.scalar_tensor_tensor(self.lo[:, k, t0:t0 + w], norm_t[:, u % 2, 0:w],
                                               modv[:, 8 * 3 * self.i + k, s:s + 1],
                                               self.hi[:, k, t0:t0 + w].bitcast(F32), ALU.add, ALU.subtract)\
                    .then_inc(self.lo_done, 1)
            for c, (t0, w) in enumerate(self.chunks):
                if not early:
                    self.inverse(dve, c)
                dve.wait_ge(self.rstd_done, self.c0 + c + 1)
                for k in range(KT):
                    u = c * KT + k
                    if self.final is not None:
                        nc.vector.scalar_tensor_tensor(self.final[:, k, t0:t0 + w], self.h[:, k, t0:t0 + w],
                                                       cols_a[:, A_GFINAL + k:A_GFINAL + k + 1],
                                                       rstd[:, t0:t0 + w], ALU.mult, ALU.mult)\
                            .then_inc(self.scaled, 1)
                        continue
                    s = 1 if t0 >= SEQ else 0
                    if u >= 2:
                        dve.wait_ge(self.lo_done, self.u0 + u - 1)
                    nc.vector.scalar_tensor_tensor(norm_t[:, u % 2, 0:w], self.h[:, k, t0:t0 + w],
                                                   coef[:, self.i, k, s:s + 1], rstd[:, t0:t0 + w],
                                                   ALU.mult, ALU.mult).then_inc(self.scaled, 1)
                    if u >= 1:
                        lo(u - 1)
                    after(u)
            if self.final is None:
                lo(n * KT - 1)

    class Ffn:
        GROUPS = D_FF // 256

        def __init__(self, tag, f, gate_i, h, norm, hid_hi, hid_lo, chunks, panel0):
            self.f, self.gate_i, self.h, self.norm = f, gate_i, h, norm
            self.hh, self.hl, self.chunks, self.panel0 = hid_hi, hid_lo, chunks, panel0
            self.up_done = sem(f"up_done_{tag}")
            self.a_free = sem(f"a_free_{tag}")
            self.b_free = sem(f"b_free_{tag}")
            self.hid_done = sem(f"hid_done_{tag}")
            self.down_done = sem(f"down_done_{tag}")
            self.down_free = sem(f"down_free_{tag}")
            self.end_panel = panel0 + 6 * self.GROUPS
            self.down_banks = (6, 7, 5) if len(chunks) == 3 else (6, 7, 2, 5)
            self.n_down = len(self.down_banks)

        def run(self, eng, body):
            with eng.Fori(0, self.GROUPS - 1) as g:
                body(g, False)
            body(self.GROUPS - 1, True)

        def panel(self, g, j):
            return (3 * g + (self.panel0 + j) // 2, (self.panel0 + j) % 2)

        def slot(self, j):
            return (self.panel0 + j) % 2

        def sp(self, sp):
            up = w_ffn_up[0, self.f].rearrange("(k p) n -> p k n", p=P)
            down = w_ffn_down[0, self.f].rearrange("(k p) n -> p k n", p=P)

            def body(g, last):
                for j in range(4):
                    col = g * 256 + (j // 2) * P + (j % 2) * D_FF
                    load_panel(sp, self.panel(g, j), raw[:, self.slot(j), :].rearrange("p (k n) -> p k n", k=KT),
                               up[:, :, bass.ds(col, P)])
                for j in range(4, 6):
                    load_panel(sp, self.panel(g, j), raw[:, self.slot(j), :].rearrange("p (k n) -> p k n", k=2),
                               down[:, bass.ds(g * 2, 2), (j - 4) * 512:(j - 3) * 512])
            self.run(sp, body)

        def pe(self, pe):
            C = len(self.chunks)

            def body(g, last):
                for j in range(4):
                    t, half = j // 2, j % 2
                    wait_panel(pe, self.panel(g, j))
                    for c, (t0, w) in enumerate(self.chunks):
                        if j == 0:
                            self.norm.normed(pe, c)
                        pe.wait_ge(self.b_free if half else self.a_free, g * (2 * C) + (t * C + c + 1))
                        if j == 1 and c == 2:
                            pe.wait_ge(self.down_free, g * (8 * C) + self.n_down)
                        o = ps[c + 3 * half][:, 0:w]
                        for k in range(KT):
                            mm = three(pe, o, wh[:, self.slot(j), k * P:(k + 1) * P],
                                       wl[:, self.slot(j), k * P:(k + 1) * P],
                                       self.norm.hi[:, k, t0:t0 + w], self.norm.lo[:, k, t0:t0 + w],
                                       k == 0, k == KT - 1)
                        mm.then_inc(self.up_done if c < C - 1 else panel_used, 1)
                for j in range(4, 6):
                    wait_panel(pe, self.panel(g, j))
                    for n in range(4):
                        for c, (t0, w) in enumerate(self.chunks):
                            i = ((j - 4) * 4 + n) * C + c
                            if j == 4 and n == 0:
                                pe.wait_ge(self.hid_done, g * (4 * C) + 2 * (C + c) + 2)
                            pe.wait_ge(self.down_free, g * (8 * C) + (i + 1))
                            o = ps[self.down_banks[i % self.n_down]][:, 0:w]
                            for k in range(2):
                                cols = slice(k * 512 + n * P, k * 512 + (n + 1) * P)
                                mm = three(pe, o, wh[:, self.slot(j), cols], wl[:, self.slot(j), cols],
                                           self.hh[:, k, t0:t0 + w], self.hl[:, k, t0:t0 + w], k == 0, k == 1)
                            mm.then_inc(self.down_done if not (n == 3 and c == C - 1) else panel_used, 1)
            self.run(pe, body)

        def wait_up(self, eng, g, t, half, c):
            C = len(self.chunks)
            if c < C - 1:
                eng.wait_ge(self.up_done, g * (4 * (C - 1)) + ((2 * t + half) * (C - 1) + c + 1))
            else:
                eng.wait_ge(panel_used, g * 6 + (self.panel0 + 2 * t + half + 1))

        def act(self, act):
            C = len(self.chunks)
            act.sem_inc(self.a_free, C)

            def body(g, last):
                for t in range(2):
                    for c, (t0, w) in enumerate(self.chunks):
                        self.wait_up(act, g, t, 0, c)
                        act.wait_ge(self.b_free, g * (2 * C) + (t * C + c + 1))
                        nc.scalar.activation(silu_a[:, c, 0:w], ps[c][:, 0:w], ACT.Silu).then_inc(self.a_free, 1)
            self.run(act, body)

        def dve(self, dve):
            C = len(self.chunks)
            dve.sem_inc(self.b_free, C)
            dve.sem_inc(self.down_free, self.n_down)

            def hidden(g, t):
                for c, (t0, w) in enumerate(self.chunks):
                    u = t * C + c
                    self.wait_up(dve, g, t, 1, c)
                    dve.wait_ge(self.a_free, g * (2 * C) + (u + C + 1))
                    nc.vector.tensor_tensor(prod[:, c % 2, 0:w], silu_a[:, c, 0:w], ps[3 + c][:, 0:w],
                                            ALU.mult).then_inc(self.b_free, 1)
                    dve.wait_ge(self.b_free, g * (2 * C) + (u + C + 1))
                    nc.vector.tensor_copy(self.hh[:, t, t0:t0 + w], prod[:, c % 2, 0:w]).then_inc(self.hid_done, 1)
                    dve.wait_ge(self.hid_done, g * (4 * C) + (2 * u + 1))
                    nc.vector.tensor_tensor(self.hl[:, t, t0:t0 + w], prod[:, c % 2, 0:w],
                                            self.hh[:, t, t0:t0 + w].bitcast(F32), ALU.subtract)\
                        .then_inc(self.hid_done, 1)

            def residual(g, j, ns):
                for n in ns:
                    for c, (t0, w) in enumerate(self.chunks):
                        i = ((j - 4) * 4 + n) * C + c
                        if n == 3 and c == C - 1:
                            dve.wait_ge(panel_used, g * 6 + (self.panel0 + j + 1))
                        else:
                            dve.wait_ge(self.down_done, g * (8 * C - 2) + (i - (j - 4) + 1))
                        s = 1 if t0 >= SEQ else 0
                        k = (j - 4) * 4 + n
                        hk = self.h[:, k, t0:t0 + w]
                        down = ps[self.down_banks[i % self.n_down]][:, 0:w]
                        nc.vector.scalar_tensor_tensor(hk, down, gates[:, self.gate_i, k, s:s + 1],
                                                       hk, ALU.mult, ALU.add).then_inc(self.down_free, 1)

            def body(g, last):
                for j in range(6):
                    if j < 4:
                        split_panel(dve, self.panel(g, j + 1))
                    if j in (1, 3):
                        hidden(g, j // 2)
                    if j == 4:
                        dve.wait_ge(self.down_free, g * (8 * C) + self.n_down)
                    if j >= 4:
                        residual(g, j, (0,))
                        if not (last and j == 5):
                            split_panel(dve, self.panel(g, j + 1))
                        residual(g, j, (1, 2, 3))
            self.run(dve, body)

        def wait_end(self, eng):
            eng.wait_ge(self.down_free, self.n_down + 8 * len(self.chunks) * self.GROUPS)

    def result_pe(pe, ready):
        for i in range(SEQ // P):
            ready(pe, i)
            for q in range(2):
                u = 2 * i + q
                if u >= 6:
                    pe.wait_ge(fin_evac_s if q else fin_evac_v, (u - 6) // 2 + 1)
                for k in range(4):
                    mm = pe.transpose(ps[2 + u % 6][:, k * P:(k + 1) * P],
                                      y_fin[:, 4 * q + k, i * P:(i + 1) * P], ident)
                mm.then_inc(fin_turned, 1)

    def result_copy(eng, q, copy, done):
        for i in range(SEQ // P):
            u = 2 * i + q
            eng.wait_ge(fin_turned, u + 1)
            copy(y_rows[:, i, q * 512:(q + 1) * 512], ps[2 + u % 6][:, :]).then_inc(done, 1)

    def result_sp(sp):
        for i in range(SEQ // P):
            sp.wait_ge(fin_evac_v, i + 1)
            sp.wait_ge(fin_evac_s, i + 1)
            sp.dma_start(out[0, i * P:(i + 1) * P, :], y_rows[:, i, :]).then_inc(out_stored[i % 2], 16)
        for b in range(2):
            sp.wait_ge(out_stored[b], 16 * (SEQ // P // 2))

    gk_f, gv_f = at("gk_f", 0, [2, TOK]), at("gv_f", 10, [4, TOK])
    k_f, v_f = at("k_f", 30, [TOK]), at("v_f", 35, [TOK])
    q_f = at("q_f", 120, [4, SEQ])
    gq_f, low_f = at("gq_f", 193, [2, SEQ]), at("low_f", 201, [TOK])
    staged = at("staged", 164, [4, 512])
    la = at("la", 40, [4, TOK])
    kk = la
    cum = at("cum", 60, [4, TOK])
    vtok = at("vtok", 80, [N_CHUNKS, GLA_HEADS * DV])
    states = at("states", 100, [2, 9, 2, DV])
    wdec = at("wdec", 148, [512])
    ktok = at("ktok", 150, [2, 256])
    last = at("last", 152, [4, N_CHUNKS])
    elast = at("elast", 152.5, [4, N_CHUNKS])
    dexp = at("dexp", 154, [2, TOK])
    gla_o = at("gla_o", 10, [GLA_HEADS, SEQ])
    eq, ek = at("eq", 140, [2, 512]), at("ek", 144, [2, 512])
    qc, kc = at("qc", 148, [2, 512]), at("kc", 152, [2, 512])
    eqs, eks = [eq, at("eq_b", 48, [2, 512])], [ek, at("ek_b", 52, [2, 512])]
    qcs, kcs = [qc, at("qc_b", 164, [2, 512])], [kc, at("kc_b", 168, [2, 512])]
    scores = at("scores", 156, [2, 4, 2, P])
    qdec = at("qdec", 40, [2, 2, 512])
    gz_s = at("gz_s", 80, [GLA_HEADS, SEQ])
    gla_r = at("gla_r", 140, [8, 512])
    gla_n = at("gla_n", 201, [2, 512])
    glah, glal = at("glah", 40, [GLA_HEADS, SEQ], F32R), at("glal", 56, [GLA_HEADS, SEQ], F32R)
    rope_t = at("rope_t", 164, [2, SEQ])
    qn, rot = at("qn", 140, [2, 512]), at("rot", 144, [2, 512])
    rot_b = at("rot_b", 148, [2, 512])
    qk_sq = at("qk_sq", 156, [2, 512])
    qk_c = at("qk_c", 205, [42, 2])
    k_r, q_r = at("k_r", 193, [10, P]), at("q_r", 104, [32, P])
    qs = at("qs", 72, [HEADS, SEQ], F32R)
    kh, kl = at("kh", 0, [KV_HEADS, TOK], F32R), at("kl", 10, [KV_HEADS, TOK], F32R)
    vv = at("vv", 20, [TOK // P, KV_HEADS, 2, HD], F32R)
    pth, ptl = at("pth", 140, [2, TOK // P, 256], F32R), at("ptl", 160, [2, TOK // P, 256], F32R)
    probs = [at("prob0", 193, [TOK]), at("prob1", 198, [TOK]), at("prob2", 34, [TOK])]
    att_t = at("att_t", 30, [2, 2, 256])
    diag = at("diag", 203, [2, P])
    mtot, nmax = at("mtot", 137, [64, 2]), at("nmax", 138.25, [64])
    rs = at("rs", 137.5, [64, 2])
    rtot, rinv = at("rtot", 138.5, [64]), at("rinv", 138.75, [64])
    ah, al = at("ah", 104, [4, SEQ], F32R), at("al", 120, [4, SEQ], F32R)
    merge_gate = at("merge_gate", 164, [2, 2, SEQ])
    ma, mb = at("ma", 193, [2, 512]), at("mb", 197, [2, 512])
    mh, ml = at("mh", 0, [KT, SEQ], F32R), at("ml", 72, [KT, SEQ], F32R)

    h_dram = nc.dram_tensor("h_saved", (P, KT, SEQ), F32, kind="Internal").ap()
    gate_dram = nc.dram_tensor("gates_saved", (20, P, SEQ), F32, kind="Internal").ap()

    win = [(C_K, P, ALL, lambda t0, w: k_f[:, t0:t0 + w]), (C_V, P, ALL, lambda t0, w: v_f[:, t0:t0 + w])]
    win += [(C_GK + i * P, P, ALL, lambda t0, w, i=i: gk_f[:, i, t0:t0 + w]) for i in range(2)]
    win += [(C_GV + i * P, P, ALL, lambda t0, w, i=i: gv_f[:, i, t0:t0 + w]) for i in range(4)]
    win += [(C_LOW, 2 * RANK, ALL, lambda t0, w: low_f[0:2 * RANK, t0:t0 + w])]
    win += [(C_Q + i * P, P, LAT, lambda t0, w, i=i: q_f[:, i, t0:t0 + w]) for i in range(4)]
    win += [(C_GQ + i * P, P, LAT, lambda t0, w, i=i: gq_f[:, i, t0:t0 + w]) for i in range(2)]
    N_KEPT = len(win)
    win += [(C_GZ + i * P, P, LAT, i) for i in range(4)]
    win += [(C_GATE + i * P, P, LAT, 4 + i) for i in range(16)]
    win_units = [(i, c) for i, (_, _, chunks, _) in enumerate(win) for c in range(len(chunks))]

    win_done, win_evac = sem("win_done"), sem("win_evac")
    saved = [sem(f"saved{i}") for i in range(4)]
    h_saved = sem("h_saved")

    def win_sp(sp, panel0, ffn0, norm):
        w = w_in[0].rearrange("(k p) n -> p k n", p=P)
        for i, (col, width, _, _) in enumerate(win):
            p = panel0 + i
            load_panel(sp, pn(p), raw[:, p % 2, 0:KT * width].rearrange("p (k n) -> p k n", k=KT),
                       w[:, :, col:col + width])
            if i == 0:
                ffn0.wait_end(sp)
                sp.dma_start(h_dram, h0[:, :, 0:SEQ]).then_inc(h_saved, 16)

    def win_pe(pe, panel0, norm):
        u = 0
        for i, (_, m, chunks, _) in enumerate(win):
            p = panel0 + i
            wait_panel(pe, pn(p))
            for c, (t0, w) in enumerate(chunks):
                if i == 0:
                    norm.normed(pe, c)
                if u >= 8:
                    pe.wait_ge(win_evac, u - 7)
                for k in range(KT):
                    cols = slice(k * m, (k + 1) * m)
                    mm = three(pe, ps[u % 8][0:m, 0:w], wh[:, p % 2, cols], wl[:, p % 2, cols],
                               norm.hi[:, k, t0:t0 + w], norm.lo[:, k, t0:t0 + w], k == 0, k == KT - 1)
                mm.then_inc(win_done if c < len(chunks) - 1 else panel_used, 1)
                u += 1

    def win_act(act, panel0):
        act.wait_ge(h_saved, 16)
        inner, kept = 0, sum(len(ch) for _, _, ch, _ in win[:N_KEPT])
        for u, (i, c) in enumerate(win_units):
            _, m, chunks, target = win[i]
            t0, w = chunks[c]
            if c < len(chunks) - 1:
                inner += 1
                act.wait_ge(win_done, inner)
            else:
                act.wait_ge(panel_used, panel0 + i + 1)
            src = ps[u % 8][0:m, 0:w]
            if i < N_KEPT:
                nc.scalar.activation(target(t0, w), src, ACT.Copy).then_inc(win_evac, 1)
                continue
            n = u - kept
            if n >= 4:
                act.wait_ge(saved[n % 4], 16 * (n // 4))
            if target < 4:
                nc.scalar.activation(staged[:, n % 4, :], src, ACT.Silu).then_inc(win_evac, 1)
            else:
                b = A_BGATE + target - 4
                nc.scalar.activation(staged[:, n % 4, :], src, ACT.Sigmoid, bias=cols_a[:, b:b + 1])\
                    .then_inc(win_evac, 1)
            act.wait_ge(win_evac, u + 1)
            act.dma_start(gate_dram[target, :, t0:t0 + w], staged[:, n % 4, :]).then_inc(saved[n % 4], 16)

    def win_dve(dve, panel0):
        for i, (_, width, _, _) in enumerate(win):
            if i >= 1:
                split_panel(dve, pn(panel0 + i), KT * width)

    dec_loaded = sem("dec_loaded")
    dec_zero = sem("dec_zero")
    g_abs, g_exp, g_ln = sem("g_abs"), sem("g_exp"), sem("g_ln")
    g_logit, g_min, g_la = sem("g_logit"), sem("g_min"), sem("g_la")
    g_scan = sem("g_scan")
    g_last, g_elast, g_diff, g_dexp, g_kk = sem("g_last"), sem("g_elast"), sem("g_diff"), sem("g_dexp"), sem("g_kk")
    g_vt, g_vcopy = sem("g_vt"), sem("g_vcopy")
    g_kt, g_kcopy, g_ds, g_state = sem("g_kt"), sem("g_kcopy"), sem("g_ds"), sem("g_state")
    dec_units = [(j, c) for j in range(4) for c in range(3)]

    def gla_setup_sp(sp):
        sp.wait_ge(panel_split, 2 * merge_p0)
        mod_load(sp, MOD_LATE)
        mod_load(sp, MOD_LATE + 1)
        sp.wait_ge(dec_zero, 1)
        sp.dma_start(wdec[0:RANK, 0:256], w_decay[0, 0]).then_inc(dec_loaded, 16)
        sp.dma_start(wdec[RANK:2 * RANK, 256:512], w_decay[0, 1]).then_inc(dec_loaded, 16)
        for n in range(4):
            sp.wait_ge(saved[n], 16 * 10)
        for p in range(MOD_LATE + 2, 2 * MOD_BLOCKS):
            mod_load(sp, p)

    steps = []
    for s in range(9):
        f = [8, 9, 0, 1, 2, 3, 4, 5, 6][s]
        b = [9, 8, 7, 6, 5, 4, 3, 2, 1][s]
        fs = [8, 0, 1, 2, 3, 4, 5, 6, 7]
        bs = [8, 7, 6, 5, 4, 3, 2, 1, 0]
        steps.append((0, f, None if s == 0 else fs[s - 1], fs[s]))
        steps.append((1, b, None if s == 0 else bs[s - 1], bs[s]))

    def gla_state_pe(pe, n_win_units):
        pe.wait_ge(win_evac, n_win_units)
        for ch in range(N_CHUNKS):
            if ch >= 2:
                pe.wait_ge(g_vcopy, ch - 1)
            for j in range(4):
                mm = pe.transpose(ps[4 + ch % 2][:, j * P:(j + 1) * P], gv_f[:, j, ch * P:(ch + 1) * P], ident)
            mm.then_inc(g_vt, 1)
        pe.wait_ge(dec_loaded, 32)
        for u, (j, c) in enumerate(dec_units):
            t0, w = ALL[c]
            if u >= 2:
                pe.wait_ge(g_min, u - 1)
            pe.matmul(ps[u % 2][:, 0:w], wdec[0:2 * RANK, j * P:(j + 1) * P], low_f[0:2 * RANK, t0:t0 + w],
                      start=True, stop=True).then_inc(g_logit, 1)
        def turn_keys(s):
            d, ch, _, _ = steps[s]
            if s >= 2:
                pe.wait_ge(g_kcopy, s - 1)
            for t in range(2):
                mm = pe.transpose(ps[s % 2][:, t * P:(t + 1) * P], kk[:, 2 * d + t, ch * P:(ch + 1) * P], ident)
            mm.then_inc(g_kt, 1)

        pe.wait_ge(g_vcopy, N_CHUNKS)
        mod_pe(pe, range(2 * MOD_GROUP, MOD_BLOCKS), range(2 * MOD_GROUP, MOD_BLOCKS))
        pe.wait_ge(g_kk, 4)
        turn_keys(0)
        pe.wait_ge(mod_evac, 3)
        for s, (_, ch, _, _) in enumerate(steps):
            if s + 1 < len(steps):
                turn_keys(s + 1)
            pe.wait_ge(g_kcopy, s + 1)
            if s >= 2:
                pe.wait_ge(g_state, s - 1)
            for hd in (0, 2, 1, 3):
                r = DK * (hd % 2)
                mm = pe.matmul(ps[2 + 2 * (s % 2) + hd % 2][r:r + DK, (hd // 2) * P:(hd // 2 + 1) * P],
                               ktok[:, s % 2, hd * DK:(hd + 1) * DK], vtok[:, ch, hd * DV:(hd + 1) * DV],
                               start=(hd < 2), stop=True, skip_group_check=True)
            mm.then_inc(g_ds, 1)

    def gla_state_act(act):
        for ch in range(N_CHUNKS):
            act.wait_ge(g_vt, ch + 1)
            nc.scalar.activation(vtok[:, ch, :], ps[4 + ch % 2][:, :], ACT.Copy).then_inc(g_vcopy, 1)
        for u, (j, c) in enumerate(dec_units):
            t0, w = ALL[c]
            b = cols_b[:, B_BDEC + j:B_BDEC + j + 1]
            act.wait_ge(g_logit, u + 1)
            nc.scalar.activation(la[:, j, t0:t0 + w], ps[u % 2][:, 0:w], ACT.Abs, bias=b).then_inc(g_abs, 1)
        for j in range(4):
            act.wait_ge(g_abs, 3 * (j + 1))
            nc.scalar.activation(la[:, j, :], la[:, j, :], ACT.Exp, scale=-1.0).then_inc(g_exp, 1)
        for j in range(4):
            act.wait_ge(g_exp, j + 1)
            nc.scalar.activation(la[:, j, :], la[:, j, :], ACT.Ln, bias=1.0).then_inc(g_ln, 1)
        act.wait_ge(g_last, 4)
        nc.scalar.activation(elast[:, :, :], last[:, :, :], ACT.Exp, scale=1.0 / GATE_NORM).then_inc(g_elast, 1)
        for j in range(4):
            act.wait_ge(g_diff, j + 1)
            nc.scalar.activation(dexp[:, j % 2, :], dexp[:, j % 2, :], ACT.Exp, scale=-1.0 / GATE_NORM)\
                .then_inc(g_dexp, 1)
        for s in range(len(steps)):
            act.wait_ge(g_kt, s + 1)
            if s >= 2:
                act.wait_ge(g_ds, s - 1)
            nc.scalar.activation(ktok[:, s % 2, :], ps[s % 2][:, 0:2 * P], ACT.Copy).then_inc(g_kcopy, 1)

    def gla_state_dve(dve):
        nc.vector.memset(wdec[0:2 * RANK, :], 0.0).then_inc(dec_zero, 1)
        for u, (j, c) in enumerate(dec_units):
            t0, w = ALL[c]
            b = cols_b[:, B_BDEC + j:B_BDEC + j + 1]
            dve.wait_ge(g_abs, u + 1)
            nc.vector.tensor_scalar(cum[:, j, t0:t0 + w], ps[u % 2][:, 0:w], b, 0.0, ALU.add, ALU.min)\
                .then_inc(g_min, 1)
        dve.wait_ge(g_min, len(dec_units))
        for j in range(4):
            dve.wait_ge(g_ln, j + 1)
            nc.vector.tensor_tensor(la[:, j, :], cum[:, j, :], la[:, j, :], ALU.subtract).then_inc(g_la, 1)
            dve.wait_ge(g_la, j + 1)
            for ch in range(N_CHUNKS):
                s = slice(ch * P, (ch + 1) * P)
                if j < 2:
                    o, i = cum[:, j, s], la[:, j, s]
                else:
                    o, i = cum[:, j, s][:, ::-1], la[:, j, s][:, ::-1]
                nc.vector.tensor_tensor_scan(o, ones, i, 0.0, ALU.mult, ALU.add).then_inc(g_scan, 1)
            mod_copy(dve, 2 * MOD_GROUP + j)
        dve.wait_ge(g_scan, 4 * N_CHUNKS)
        for j in range(4):
            v = cum[:, j, :].rearrange("p (n t) -> p n t", t=P)
            nc.vector.tensor_copy(last[:, j, :], v[:, :, P - 1] if j < 2 else v[:, :, 0]).then_inc(g_last, 1)
        dve.wait_ge(g_last, 4)

        def decayed_keys(j):
            dve.wait_ge(g_dexp, j + 1)
            nc.vector.tensor_tensor(kk[:, j, :], dexp[:, j % 2, :], gk_f[:, j % 2, :], ALU.mult).then_inc(g_kk, 1)
        for j in range(4):
            v = cum[:, j, :].rearrange("p (n t) -> p n t", t=P)
            if j >= 2:
                dve.wait_ge(g_kk, j - 1)
            nc.vector.tensor_tensor(dexp[:, j % 2, :].rearrange("p (n t) -> p n t", t=P), v,
                                    last[:, j, :].unsqueeze(2).to_broadcast([P, N_CHUNKS, P]),
                                    ALU.subtract).then_inc(g_diff, 1)
            if j >= 1:
                decayed_keys(j - 1)
        decayed_keys(3)
        for n in range(2 * MOD_GROUP + 4, MOD_BLOCKS):
            mod_copy(dve, n)
        mod_finish(dve, 2)
        dve.wait_ge(g_elast, 1)
        for s, (d, ch, src, dst) in enumerate(steps):
            dve.wait_ge(g_ds, s + 1)
            if s >= 2:
                dve.wait_ge(g_half, 2 * (s - 1))
            for t in range(2):
                for par in range(2):
                    r = slice(DK * par, DK * par + DK)
                    ds = ps[2 + 2 * (s % 2) + par][r, t * P:(t + 1) * P]
                    done = g_state if (t, par) == (1, 1) else g_half
                    if src is None:
                        nc.vector.tensor_copy(states[r, d, dst, t, :], ds).then_inc(done, 1)
                    else:
                        nc.vector.scalar_tensor_tensor(states[r, d, dst, t, :], states[r, d, src, t, :],
                                                       elast[r, 2 * d + t, ch:ch + 1], ds, ALU.mult, ALU.add)\
                            .then_inc(done, 1)

    g_half = sem("g_half")

    g_lq, g_eq, g_qk, g_sc, g_pred, g_oz, g_oc = (sem("g_lq"), sem("g_eq"), sem("g_qk"), sem("g_sc"), sem("g_pred"),
                                                  sem("g_oz"), sem("g_oc"))
    g_qd, g_qde = sem("g_qd"), sem("g_qde")
    N_SCORES = N_LEVELS + 1

    def bank_of(par, cc):
        return 2 * (cc // 2) + par

    def gla_intra_pe(pe):
        for hf in range(2):
            for lv in range(N_SCORES):
                g = hf * N_SCORES + lv
                pe.wait_ge(g_qk, 2 * g + 2)
                if g >= 2:
                    pe.wait_ge(g_pred, 4 * (g - 1))
                if lv == 1 and hf > 0:
                    pe.wait_ge(g_oc, 4 * hf)
                if g == 0:
                    pe.wait_ge(g_state, len(steps))
                for cc in range(4):
                    for hd in range(GLA_HEADS):
                        r, t, par = slice(DK * (hd % 2), DK * (hd % 2) + DK), hd // 2, hd % 2
                        tok = slice(cc * P, (cc + 1) * P)
                        lat = slice(hf * 512 + cc * P, hf * 512 + (cc + 1) * P)
                        w = gk_f[r, t, lat] if lv == 0 else kcs[lv % 2][r, t, tok]
                        col = ((cc % 2) * 2 + t) * P
                        mm = pe.matmul(ps[4 * (lv % 2) + bank_of(par, cc)][:, col:col + P], w, qcs[lv % 2][r, t, tok],
                                       start=True, stop=True)
                mm.then_inc(g_sc, 1)
            pe.wait_ge(g_pred, 4 * N_SCORES * (hf + 1))
            pe.wait_ge(g_qd, 2 * (hf + 1))
            if hf > 0:
                pe.wait_ge(g_oc, 4 * hf)
            for cc in range(4):
                ch = 4 * hf + cc
                for hd in range(GLA_HEADS):
                    r, t, par = slice(DK * (hd % 2), DK * (hd % 2) + DK), hd // 2, hd % 2
                    o = ps[4 + bank_of(par, cc)][:, ((cc % 2) * 2 + t) * P:((cc % 2) * 2 + t + 1) * P]
                    pe.matmul(o, vtok[:, ch, hd * DV:(hd + 1) * DV], scores[:, par, cc, t, :],
                              start=True, stop=False)
                    for d in range(2):
                        mm = pe.matmul(o, states[r, d, ch, t, :], qdec[r, d, t, cc * P:(cc + 1) * P],
                                       start=False, stop=(d == 1))
            mm.then_inc(g_oz, 1)

    def gla_intra_act(act):
        for hf in range(2):
            for d in range(2):
                if hf > 0:
                    act.wait_ge(g_oz, hf)
                tok = slice(hf * 512, (hf + 1) * 512)
                act.wait_ge(g_kt, len(steps))
                nc.scalar.activation(qdec[:, d, :, :], cum[:, 2 * d:2 * d + 2, tok], ACT.Exp,
                                     scale=1.0 / GATE_NORM).then_inc(g_qde, 1)
            for lv in range(1, N_SCORES):
                g = hf * N_LEVELS + lv - 1
                act.wait_ge(g_lq, 4 * g + 4)
                for e in (eqs[lv % 2], eks[lv % 2]):
                    nc.scalar.activation(e[:, :, :], e[:, :, :], ACT.Exp, scale=1.0 / GATE_NORM).then_inc(g_eq, 1)

    def gla_intra_dve(dve):
        dve.wait_ge(g_state, len(steps))

        def outputs(hf):
            dve.wait_ge(g_oz, hf + 1)
            for cp in range(2):
                for par in range(2):
                    src = ps[4 + 2 * cp + par][:, :].rearrange("p (c t i) -> p t c i", c=2, t=2)
                    dst = gla_o[:, par::2, hf * 512 + cp * 256:hf * 512 + cp * 256 + 256]\
                        .rearrange("p t (c i) -> p t c i", c=2)
                    nc.vector.tensor_copy(dst, src).then_inc(g_oc, 1)

        for n in range(4):
            dve.wait_ge(saved[n], 16 * 10)
        for hf in range(2):
            tok = slice(hf * 512, (hf + 1) * 512)
            if hf > 0:
                dve.wait_ge(g_sc, hf * N_SCORES)
            nc.vector.tensor_scalar(qc[:, :, :], gq_f[:, :, tok], 2 * DK ** -0.5, None, ALU.mult).then_inc(g_qk, 2)

            def differences(lv):
                g = hf * N_LEVELS + lv - 1
                if lv >= 3 or hf > 0:
                    dve.wait_ge(g_qk, 2 * (hf * N_SCORES + lv - 1))
                s = CHUNK >> lv

                def halves(a):
                    v = a.rearrange("p t (n r s) -> p t n r s", r=2, s=s)
                    return v[:, :, :, 0, :], v[:, :, :, 1, :]
                fl, fr = halves(cum[:, 0:2, tok])
                bl, br = halves(cum[:, 2:4, tok])
                ql, qr = halves(eqs[lv % 2][:, :, :])
                kl_, kr_ = halves(eks[lv % 2][:, :, :])
                n = 512 // (2 * s)
                fref = fl[:, :, :, s - 1:s].to_broadcast([P, 2, n, s])
                bref = br[:, :, :, 0:1].to_broadcast([P, 2, n, s])
                nc.vector.tensor_tensor(qr, fr, fref, ALU.subtract).then_inc(g_lq, 1)
                nc.vector.tensor_tensor(ql, bl, bref, ALU.subtract).then_inc(g_lq, 1)
                nc.vector.tensor_tensor(kl_, fref, fl, ALU.subtract).then_inc(g_lq, 1)
                nc.vector.tensor_tensor(kr_, bref, br, ALU.subtract).then_inc(g_lq, 1)

            def products(lv):
                g = hf * N_LEVELS + lv - 1
                dve.wait_ge(g_eq, 2 * g + 2)
                if lv >= 2 or hf > 0:
                    dve.wait_ge(g_sc, hf * N_SCORES + lv - 1)
                nc.vector.scalar_tensor_tensor(qcs[lv % 2][:, :, :], gq_f[:, :, tok], DK ** -0.5,
                                               eqs[lv % 2][:, :, :], ALU.mult, ALU.mult).then_inc(g_qk, 1)
                nc.vector.tensor_tensor(kcs[lv % 2][:, :, :], gk_f[:, :, tok], eks[lv % 2][:, :, :], ALU.mult)\
                    .then_inc(g_qk, 1)

            def take(lv):
                g = hf * N_SCORES + lv
                dve.wait_ge(g_sc, g + 1)
                for b in range(4):
                    par, cp = b % 2, b // 2
                    dst = scores[:, par, 2 * cp:2 * cp + 2, :, :].rearrange("p c t i -> p (c t) i")
                    src = ps[4 * (lv % 2) + b][:, :].rearrange("p (n i) -> p n i", i=P)
                    if lv == 0:
                        if hf > 0:
                            dve.wait_ge(g_oz, hf)
                        nc.vector.tensor_copy(dst, src).then_inc(g_pred, 1)
                    else:
                        dve.wait_ge(g_pred, 4 * g + b - 3)
                        m = cst[:, K_MASK + lv - 1:K_MASK + lv, :].bitcast(I32).to_broadcast([P, 4, P])
                        nc.vector.copy_predicated(dst, m, src).then_inc(g_pred, 1)
            differences(1)
            differences(2)
            if hf > 0:
                outputs(hf - 1)
            for d in range(2):
                dve.wait_ge(g_qde, 2 * hf + d + 1)
                nc.vector.scalar_tensor_tensor(qdec[:, d, :, :], gq_f[:, :, tok], DK ** -0.5, qdec[:, d, :, :],
                                               ALU.mult, ALU.mult).then_inc(g_qd, 1)
            for lv in range(N_SCORES):
                if lv + 1 < N_SCORES:
                    products(lv + 1)
                if lv + 3 < N_SCORES:
                    differences(lv + 3)
                take(lv)
        outputs(1)

    z_loaded, o_sq, o_ss, o_ln, o_rs, o_norm, o_gate, o_hi, o_lo = (
        sem(n) for n in ("z_loaded", "o_sq", "o_ss", "o_ln", "o_rs", "o_norm", "o_gate", "o_hi", "o_lo"))
    o_units = [(hd, c) for hd in range(GLA_HEADS) for c in range(2)]

    def gla_out_sp(sp):
        for n in range(4):
            sp.wait_ge(saved[n], 16 * 10)
        sp.wait_ge(g_oz, 2)
        sp.dma_start(gz_s[:, :, :], gate_dram[0:4].rearrange("n p t -> p n t")).then_inc(z_loaded, 16)

    def gla_out_act(act):
        def square(u):
            hd, c = o_units[u]
            if u >= 2:
                act.wait_ge(o_ss, u - 1)
            nc.scalar.activation(sq[:, u % 2, :], gla_o[:, hd, c * 512:(c + 1) * 512], ACT.Square).then_inc(o_sq, 1)
        act.wait_ge(g_oc, 8)
        square(0)
        for u in range(8):
            if u < 7:
                square(u + 1)
            act.wait_ge(o_ss, u + 1)
            nc.scalar.activation(gla_r[:, u, :], ps[u % 4][:, :], ACT.Ln, bias=eps, scale=1.0 / DV).then_inc(o_ln, 1)
        for half in range(2):
            act.wait_ge(o_ln, 4 * half + 4)
            r = gla_r[:, 4 * half:4 * half + 4, :]
            nc.scalar.activation(r, r, ACT.Exp, scale=-0.5).then_inc(o_rs, 1)

    def gla_out_pe(pe):
        for u in range(8):
            pe.wait_ge(o_sq, u + 1)
            if u >= 4:
                pe.wait_ge(o_ln, u - 3)
            pe.matmul(ps[u % 4][:, :], ones, sq[:, u % 2, :], start=True, stop=True).then_inc(o_ss, 1)

    def gla_out_dve(dve):
        dve.wait_ge(z_loaded, 16)
        for u, (hd, c) in enumerate(o_units):
            t = slice(c * 512, (c + 1) * 512)
            dve.wait_ge(o_rs, u // 4 + 1)
            nc.vector.scalar_tensor_tensor(gla_n[:, 0, :], gla_o[:, hd, t], cols_b[:, B_GGLA:B_GGLA + 1],
                                           gla_r[:, u, :], ALU.mult, ALU.mult).then_inc(o_norm, 1)
            dve.wait_ge(o_norm, u + 1)
            nc.vector.tensor_tensor(gla_n[:, 1, :], gla_n[:, 0, :], gz_s[:, hd, t], ALU.mult).then_inc(o_gate, 1)
            dve.wait_ge(o_gate, u + 1)
            nc.vector.tensor_copy(glah[:, hd, t], gla_n[:, 1, :]).then_inc(o_hi, 1)
            dve.wait_ge(o_hi, u + 1)
            nc.vector.tensor_tensor(glal[:, hd, t], gla_n[:, 1, :], glah[:, hd, t].bitcast(F32), ALU.subtract)\
                .then_inc(o_lo, 1)

    qk_units = [("k", 0, c) for c in range(3)] + [("q", t, c) for t in range(4) for c in range(2)]
    rotated_units = [u for u, (_, _, c) in enumerate(qk_units) if c < 2]
    qk_copies = [4 if kind == "k" else 2 for kind, _, _ in qk_units]
    qk_blocks = [(4 * c if kind == "k" else 10 + 8 * t + 4 * c, 4 * c if kind == "k" else 8 * t + 4 * c, ALL[c][1] // P)
                 for kind, t, c in qk_units]
    rope_loaded, k_sq, k_ss, k_root, k_inv, k_spread, k_r_done, k_norm, k_perm, k_a, k_b, k_rot, k_hi, k_lo = (
        sem(n) for n in ("rope_loaded", "k_sq", "k_ss", "k_root", "k_inv", "k_spread", "k_r_done", "k_norm",
                         "k_perm", "k_a", "k_b",
                         "k_rot", "k_hi", "k_lo"))
    v_turned, v_hi, v_lo = sem("v_turned"), sem("v_hi"), sem("v_lo")

    def qk_src(unit):
        kind, t, c = unit
        t0, w = ALL[c]
        if kind == "k":
            return k_f[:, t0:t0 + w], t0, w
        return q_f[:, t, t0:t0 + w], t0, w

    def qk_sp(sp):
        sp.dma_start(rope_t[:, :, :], rope.rearrange("a p t -> p a t")).then_inc(rope_loaded, 16)

    def qk_act(act):
        def square(u):
            src, _, w = qk_src(qk_units[u])
            if u >= 2:
                act.wait_ge(k_ss, u - 1)
            nc.scalar.activation(qk_sq[:, u % 2, 0:w], src, ACT.Square).then_inc(k_sq, 1)
        for u in range(len(qk_units)):
            square(u)
        act.wait_ge(k_ss, len(qk_units))
        nc.scalar.activation(qk_c[:, :, :], ps[0][:, 0:84].rearrange("p (n h) -> p n h", h=2), ACT.Sqrt,
                             bias=eps, scale=1.0 / HD).then_inc(k_root, 1)
        act.wait_ge(k_inv, 1)
        for dst, n0, n in ((k_r[:, :, :], 0, 10), (q_r[:, 0:16, :], 10, 16), (q_r[:, 16:32, :], 26, 16)):
            nc.scalar.activation(dst.rearrange("p n (h d) -> p n h d", h=2),
                                 qk_c[:, n0:n0 + n, :].unsqueeze(3).to_broadcast([P, n, 2, HD]), ACT.Copy)\
                .then_inc(k_spread, 1)
        for u, (kind, t, c) in enumerate(qk_units):
            t0, w = ALL[c]
            act.wait_ge(k_rot, u + 1)
            for half in range(2):
                own = slice(HD * half, HD * half + HD)
                other = slice(HD * (1 - half), HD * (1 - half) + HD)
                r = rot[own, u % 2, 0:w]
                if kind == "q":
                    nc.scalar.activation(qs[own, 2 * t + half, t0:t0 + w], r, ACT.Copy).then_inc(k_hi, 1)
                else:
                    for o in (own, other):
                        nc.scalar.activation(kh[o, half, t0:t0 + w], r, ACT.Copy).then_inc(k_hi, 1)

    def qk_pe(pe):
        pe.wait_ge(o_ln, 8)
        for u, (n0, _, n) in enumerate(qk_blocks):
            pe.wait_ge(k_sq, u + 1)
            for b in range(n):
                mm = pe.matmul(ps[0][:, 2 * (n0 + b):2 * (n0 + b) + 2], qk_sq[:, u % 2, b * P:(b + 1) * P],
                               cst[:, K_BLK, ::HD], start=True, stop=True)
            mm.then_inc(k_ss, 1)
        for n in range(3):
            for b in range(4 if n < 2 else 2):
                kt = 4 * n + b
                mm = pe.transpose(ps[4 + n][:, b * P:(b + 1) * P], v_f[:, kt * P:(kt + 1) * P], ident)
            mm.then_inc(v_turned, 1)
        pe.wait_ge(v_lo, 3)

        def spread(u):
            kind, t, c = qk_units[u]
            _, n0, n = qk_blocks[u]
            pe.wait_ge(k_spread, 1 if kind == "k" else 2 + t // 2)
            if u - 4 in rotated_units:
                pe.wait_ge(k_norm, rotated_units.index(u - 4) + 1)
            elif u >= 4:
                pe.wait_ge(k_rot, u - 3)
            for b in range(n):
                w = (k_r if kind == "k" else q_r)[:, n0 + b, :]
                mm = pe.matmul(ps[u % 4][:, b * P:(b + 1) * P], w, ident, start=True, stop=True)
            mm.then_inc(k_r_done, 1)

        for u in range(4):
            spread(u)
        m = 0
        for u in range(len(qk_units)):
            if u in rotated_units:
                pe.wait_ge(k_norm, m + 1)
                if m >= 2:
                    pe.wait_ge(k_b, m - 1)
                pe.matmul(ps[6 + m % 2][:, :], cst[:, K_PERM, :], qn[:, m % 2, :], start=True, stop=True)\
                    .then_inc(k_perm, 1)
                m += 1
            if u + 4 < len(qk_units):
                spread(u + 4)

    def qk_dve(dve):
        dve.wait_ge(k_root, 1)
        nc.vector.reciprocal(qk_c[:, :, :], qk_c[:, :, :]).then_inc(k_inv, 1)
        dve.wait_ge(o_lo, 8)
        for n in range(3):
            m = 4 if n < 2 else 2
            src = ps[4 + n][:, 0:m * P].rearrange("p (b g d) -> p b g d", b=m, g=2)
            dve.wait_ge(v_turned, n + 1)
            nc.vector.tensor_copy(vv[:, 4 * n:4 * n + m, :, 0, :], src).then_inc(v_hi, 1)
            dve.wait_ge(v_hi, n + 1)
            nc.vector.tensor_tensor(vv[:, 4 * n:4 * n + m, :, 1, :], src,
                                    vv[:, 4 * n:4 * n + m, :, 0, :].bitcast(F32), ALU.subtract).then_inc(v_lo, 1)

        def low(u):
            kind, t, c = qk_units[u]
            t0, w = ALL[c]
            dve.wait_ge(k_hi, sum(qk_copies[:u + 1]))
            for half in range(2):
                own = slice(HD * half, HD * half + HD)
                other = slice(HD * (1 - half), HD * (1 - half) + HD)
                r = rot[own, u % 2, 0:w]
                if kind == "q":
                    hd = 2 * t + half
                    nc.vector.tensor_tensor(qs[other, hd, t0:t0 + w], r, qs[own, hd, t0:t0 + w].bitcast(F32),
                                            ALU.subtract).then_inc(k_lo, 1)
                else:
                    for o in (own, other):
                        nc.vector.tensor_tensor(kl[o, half, t0:t0 + w], r, kh[own, half, t0:t0 + w].bitcast(F32),
                                                ALU.subtract).then_inc(k_lo, 1)

        dve.wait_ge(rope_loaded, 16)

        def normed(u, dst, done):
            kind = qk_units[u][0]
            src, _, w = qk_src(qk_units[u])
            g = cols_b[:, (B_GK if kind == "k" else B_GQ):(B_GK if kind == "k" else B_GQ) + 1]
            dve.wait_ge(k_r_done, u + 1)
            nc.vector.scalar_tensor_tensor(dst, src, g, ps[u % 4][:, 0:w], ALU.mult, ALU.mult).then_inc(done, 1)

        def rotate(u):
            m = rotated_units.index(u)
            _, t0, w = qk_src(qk_units[u])
            dve.wait_ge(k_norm, m + 1)
            if u >= 2:
                dve.wait_ge(k_lo, sum(qk_copies[:u - 1]))
            nc.vector.tensor_tensor(rot[:, u % 2, 0:w], qn[:, m % 2, 0:w], rope_t[:, 0, t0:t0 + w], ALU.mult)\
                .then_inc(k_a, 1)
            if u >= 1:
                low(u - 1)
            dve.wait_ge(k_perm, m + 1)
            nc.vector.tensor_tensor(rot_b[:, m % 2, 0:w], ps[6 + m % 2][:, 0:w], rope_t[:, 1, t0:t0 + w],
                                    ALU.mult).then_inc(k_b, 1)
            dve.wait_ge(k_a, m + 1)
            dve.wait_ge(k_b, m + 1)
            nc.vector.tensor_tensor(rot[:, u % 2, 0:w], rot[:, u % 2, 0:w], rot_b[:, m % 2, 0:w], ALU.add)\
                .then_inc(k_rot, 1)

        normed(0, qn[:, 0, :], k_norm)
        for u, (_, _, c) in enumerate(qk_units):
            if u + 1 in rotated_units:
                normed(u + 1, qn[:, rotated_units.index(u + 1) % 2, :], k_norm)
            if u in rotated_units:
                rotate(u)
            else:
                dve.wait_ge(k_lo, sum(qk_copies[:u - 1]))
                normed(u, rot[:, u % 2, 0:ALL[c][1]], k_rot)
                low(u - 1)
        low(len(qk_units) - 1)

    N_K_LO = sum(qk_copies)

    s_lat, s_ctx, mx_done, nm_done, exp_lat, exp_ctx, rt_done, ri_done, dg_done = (
        sem(n) for n in ("s_lat", "s_ctx", "mx_done", "nm_done", "exp_lat", "exp_ctx", "rt_done", "ri_done", "dg_done"))
    t_done, p_hi, p_lo, pv_done = (sem(n) for n in ("t_done", "p_hi", "p_lo", "pv_done"))
    ot_done, os_done, a_hi, a_lo = (sem(n) for n in ("ot_done", "os_done", "a_hi", "a_lo"))
    Q_BLOCKS = SEQ // P
    N_STEP = HEADS * Q_BLOCKS
    N_PAIR = N_STEP // 2
    TGROUPS = [(0, 4), (4, 8), (8, 10)]
    TG = len(TGROUPS)
    K_TILES = TOK // P

    def latent_scores(i):
        return psum[:, SEQ * (i % 2):SEQ * (i % 2 + 1)]

    context_scores = ps[4][:, 0:CTX]

    def turned_of(i, r):
        a, b = TGROUPS[r]
        return ps[5 + (TG * i + r) % 2][:, 0:(b - a) * P]

    def att_pe(pe):
        pe.wait_ge(k_lo, N_K_LO)
        pe.wait_ge(v_lo, 3)

        def score(i, context):
            hd, qt = divmod(i, Q_BLOCKS)
            kv = hd // (HEADS // KV_HEADS)
            if context and i >= 1:
                pe.wait_ge(exp_ctx, i)
            if not context and i >= 2:
                pe.wait_ge(exp_lat, i - 1)
            for t0, w in ALL[2:] if context else LAT:
                o = context_scores if context else latent_scores(i)[:, t0:t0 + w]
                q = qs[:, hd, qt * P:(qt + 1) * P]
                pe.matmul(o, q, kh[:, kv, t0:t0 + w], start=True, stop=False)
                mm = pe.matmul(o, q, kl[:, kv, t0:t0 + w], start=False, stop=True)
            mm.then_inc(s_ctx if context else s_lat, 1)

        def turn(i, groups):
            pe.wait_ge(exp_lat, i + 1)
            pe.wait_ge(dg_done, i + 1)
            for r in groups:
                a, b = TGROUPS[r]
                n = TG * i + r
                if n >= 2:
                    pe.wait_ge(p_lo, n - 1)
                for kt in range(a, b):
                    mm = pe.matmul(turned_of(i, r)[:, (kt - a) * P:(kt - a + 1) * P],
                                   probs[i % 3][:, kt * P:(kt + 1) * P], diag[:, i % 2, :], start=True, stop=True)
                mm.then_inc(t_done, 1)

        def values(v, tiles):
            kv = 2 * v // Q_BLOCKS // (HEADS // KV_HEADS)
            pe.wait_ge(p_lo, 2 * TG * (v + 1))
            if v >= 1:
                pe.wait_ge(os_done, v)
            o = ps[7][:, 0:256]
            for kt in tiles:
                w = vv[:, kt, kv, :, :].rearrange("p a d -> p (a d)")
                pe.matmul(o, w, pth[:, v % 2, kt, :], start=(kt == 0), stop=False)
                mm = pe.matmul(o, w, ptl[:, v % 2, kt, :], start=False, stop=(kt == K_TILES - 1))
            if K_TILES - 1 in tiles:
                mm.then_inc(pv_done, 1)

        score(0, False)
        score(0, True)
        score(1, False)
        for i in range(N_STEP + 4):
            if 2 <= i < N_STEP + 2:
                turn(i - 2, (2,))
            if i + 1 < N_STEP:
                score(i + 1, True)
            if i >= 4:
                values((i - 4) // 2, range(5, K_TILES) if i % 2 else range(0, 5))
            if 1 <= i <= N_STEP:
                turn(i - 1, (0, 1))
            if i + 2 < N_STEP:
                score(i + 2, False)

    def att_act(act):
        def exp_context(i):
            act.wait_ge(nm_done, i + 1)
            if i >= 3:
                act.wait_ge(t_done, TG * (i - 2))
            nc.scalar.activation(probs[i % 3][:, SEQ:TOK], context_scores, ACT.Exp, bias=nmax[:, i:i + 1],
                                 scale=SCALE, accum_out=rs[:, i, 1:2]).then_inc(exp_ctx, 1)

        def exp_latent(i):
            nc.scalar.activation(probs[i % 3][:, 0:SEQ], latent_scores(i), ACT.Exp, bias=nmax[:, i:i + 1],
                                 scale=SCALE, accum_out=rs[:, i, 0:1]).then_inc(exp_lat, 1)

        def high(i, groups):
            v = i // 2
            if v >= 2:
                act.wait_ge(pv_done, v - 1)
            for r in groups:
                a, b = TGROUPS[r]
                act.wait_ge(t_done, TG * i + r + 1)
                nc.scalar.activation(pth[:, v % 2, a:b, (i % 2) * P:(i % 2 + 1) * P],
                                     turned_of(i, r).rearrange("p (k q) -> p k q", q=P), ACT.Copy).then_inc(p_hi, 1)

        def fold(v):
            act.wait_ge(pv_done, v + 1)
            if v >= 2:
                act.wait_ge(os_done, v - 1)
            nc.scalar.activation(att_t[0:HD, 0, v % 2, :], ps[7][HD:P, 0:256], ACT.Copy)\
                .then_inc(ot_done, 1)

        for i in range(N_STEP + 4):
            if i < N_STEP:
                exp_context(i)
            if 2 <= i < N_STEP + 2:
                high(i - 2, (2,))
            if i < N_STEP:
                exp_latent(i)
            if i >= 5 and i % 2 == 1:
                fold((i - 5) // 2)
            if 1 <= i <= N_STEP:
                high(i - 1, (0, 1))

    def att_dve(dve):
        def maxima(i):
            dve.wait_ge(s_lat, i + 1)
            nc.vector.reduce_max(mtot[:, i, 0:1], latent_scores(i), AX_X).then_inc(mx_done, 1)
            dve.wait_ge(s_ctx, i + 1)
            nc.vector.reduce_max(mtot[:, i, 1:2], context_scores, AX_X).then_inc(mx_done, 1)

        def bias(i):
            dve.wait_ge(mx_done, 2 * (i + 1))
            nc.vector.tensor_scalar(nmax[:, i:i + 1], mtot[:, i, 0:1], mtot[:, i, 1:2], -SCALE, ALU.max, ALU.mult)\
                .then_inc(nm_done, 1)

        def low(i, r):
            v = i // 2
            a, b = TGROUPS[r]
            q = slice((i % 2) * P, (i % 2 + 1) * P)
            dve.wait_ge(p_hi, TG * i + r + 1)
            nc.vector.tensor_tensor(ptl[:, v % 2, a:b, q], turned_of(i, r).rearrange("p (k q) -> p k q", q=P),
                                    pth[:, v % 2, a:b, q].bitcast(F32), ALU.subtract).then_inc(p_lo, 1)

        def total(i):
            dve.wait_ge(exp_ctx, i + 1)
            dve.wait_ge(exp_lat, i + 1)
            nc.vector.tensor_tensor(rtot[:, i:i + 1], rs[:, i, 0:1], rs[:, i, 1:2], ALU.add).then_inc(rt_done, 1)

        def inverse(i):
            dve.wait_ge(rt_done, i + 1)
            nc.vector.reciprocal(rinv[:, i:i + 1], rtot[:, i:i + 1]).then_inc(ri_done, 1)

        def diagonal(i):
            dve.wait_ge(ri_done, i + 1)
            if i >= 2:
                dve.wait_ge(t_done, TG * (i - 1))
            nc.vector.tensor_scalar(diag[:, i % 2, :], ident, rinv[:, i:i + 1], None, ALU.mult).then_inc(dg_done, 1)

        def finish(v, stage):
            hd, qb = divmod(v, Q_BLOCKS // 2)
            rows = slice(HD * (hd % 2), HD * (hd % 2) + HD)
            q = slice(qb * 256, (qb + 1) * 256)
            if stage == 0:
                dve.wait_ge(ot_done, v + 1)
                nc.vector.tensor_tensor(att_t[rows, 1, v % 2, :], ps[7][0:HD, 0:256],
                                        att_t[0:HD, 0, v % 2, :], ALU.add).then_inc(os_done, 1)
            elif stage == 1:
                dve.wait_ge(os_done, v + 1)
                nc.vector.tensor_copy(ah[rows, hd // 2, q], att_t[rows, 1, v % 2, :]).then_inc(a_hi, 1)
            else:
                dve.wait_ge(a_hi, v + 1)
                nc.vector.tensor_tensor(al[rows, hd // 2, q], att_t[rows, 1, v % 2, :],
                                        ah[rows, hd // 2, q].bitcast(F32), ALU.subtract).then_inc(a_lo, 1)

        for i in range(N_STEP + 5):
            before = 1 <= i <= N_STEP
            if i < N_STEP:
                maxima(i)
            if before:
                total(i - 1)
            if i < N_STEP:
                bias(i)
            if before:
                inverse(i - 1)
            for r in range(TG):
                if 2 <= i < N_STEP + 2:
                    low(i - 2, r)
                if r == 0 and before:
                    diagonal(i - 1)
                if i >= 6 and i % 2 == 0:
                    finish((i - 6) // 2, r)

    gate_loaded = [sem("gate_loaded0"), sem("gate_loaded1")]
    m_done, m_t1, m_t2, m_sum, m_hi, m_lo = (sem(n) for n in ("m_done", "m_t1", "m_t2", "m_sum", "m_hi", "m_lo"))
    w_done, w_res = sem("w_done"), sem("w_res")
    h_back = sem("h_back")

    def merge_sp(sp, panel0):
        wb = w_branch[0].rearrange("b (k p) n -> p (b k) n", p=P)
        sp.wait_ge(pv_done, N_PAIR)
        for n in range(KT):
            load_panel(sp, pn(panel0 + n), raw[:, (panel0 + n) % 2, :].rearrange("p (k n) -> p k n", k=KT),
                       wb[:, :, n * P:(n + 1) * P])
            if n >= 2:
                sp.wait_ge(m_t2, 2 * (n - 1))
            sp.dma_start(merge_gate[:, n % 2, :, :],
                         gate_dram[4:20].rearrange("(b n) p t -> p b n t", b=2)[:, :, n, :])\
                .then_inc(gate_loaded[n % 2], 16)
        wo = w_out[0].rearrange("(k p) n -> p k n", p=P)
        for n in range(KT):
            load_panel(sp, pn(panel0 + KT + n), raw[:, (panel0 + KT + n) % 2, :].rearrange("p (k n) -> p k n", k=KT),
                       wo[:, :, n * P:(n + 1) * P])
            if n == 0:
                sp.wait_ge(panel_used, panel0 + KT)
                sp.wait_ge(h_saved, 16)
                sp.dma_start(h1[:, :, :], h_dram).then_inc(h_back, 16)

    def merge_pe(pe, panel0):
        pe.wait_ge(a_lo, N_PAIR)
        for n in range(KT):
            p = panel0 + n
            wait_panel(pe, pn(p))
            for b, (hi, lo) in enumerate(((ah, al), (glah, glal))):
                for c, (t0, w) in enumerate(LAT):
                    u = 4 * n + 2 * b + c
                    if u >= 8:
                        pe.wait_ge(m_t2 if b else m_t1, 2 * (n - 2) + c + 1)
                    for k in range(4):
                        cols = slice((4 * b + k) * P, (4 * b + k + 1) * P)
                        mm = three(pe, ps[u % 8][:, :], wh[:, p % 2, cols], wl[:, p % 2, cols],
                                   hi[:, k, t0:t0 + w], lo[:, k, t0:t0 + w], k == 0, k == 3)
                    mm.then_inc(m_done if (b, c) != (1, 1) else panel_used, 1)
        pe.wait_ge(m_lo, 16)
        for n in range(KT):
            p = panel0 + KT + n
            wait_panel(pe, pn(p))
            for c, (t0, w) in enumerate(LAT):
                u = 2 * n + c
                if u >= 8:
                    pe.wait_ge(w_res, u - 7)
                for k in range(KT):
                    cols = slice(k * P, (k + 1) * P)
                    mm = three(pe, ps[u % 8][:, :], wh[:, p % 2, cols], wl[:, p % 2, cols],
                               mh[:, k, t0:t0 + w], ml[:, k, t0:t0 + w], k == 0, k == KT - 1)
                mm.then_inc(w_done if c == 0 else panel_used, 1)

    def merge_dve(dve, panel0):
        split_panel(dve, pn(panel0))
        for n in range(KT):
            p = panel0 + n
            split_panel(dve, pn(p + 1))
            dve.wait_ge(gate_loaded[n % 2], 16 * (n // 2 + 1))
            for b in range(2):
                for c, (t0, w) in enumerate(LAT):
                    if (b, c) == (1, 1):
                        dve.wait_ge(panel_used, p + 1)
                    else:
                        dve.wait_ge(m_done, 3 * n + 2 * b + c + 1)
                    nc.vector.tensor_tensor((mb if b else ma)[:, c, :], ps[(4 * n + 2 * b + c) % 8][:, :],
                                            merge_gate[:, n % 2, b, t0:t0 + w], ALU.mult)\
                        .then_inc(m_t2 if b else m_t1, 1)
            for c, (t0, w) in enumerate(LAT):
                u = 2 * n + c
                dve.wait_ge(m_t2, u + 1)
                dve.wait_ge(m_t1, u + 1)
                nc.vector.tensor_tensor(ma[:, c, :], ma[:, c, :], mb[:, c, :], ALU.add).then_inc(m_sum, 1)
                dve.wait_ge(m_sum, u + 1)
                nc.vector.tensor_copy(mh[:, n, t0:t0 + w], ma[:, c, :]).then_inc(m_hi, 1)
                dve.wait_ge(m_hi, u + 1)
                nc.vector.tensor_tensor(ml[:, n, t0:t0 + w], ma[:, c, :], mh[:, n, t0:t0 + w].bitcast(F32),
                                        ALU.subtract).then_inc(m_lo, 1)
        for n in range(KT):
            p = panel0 + KT + n
            if n + 1 < KT:
                split_panel(dve, pn(p + 1))
            if n == 0:
                dve.wait_ge(h_back, 16)
            for c, (t0, w) in enumerate(LAT):
                if c == 0:
                    dve.wait_ge(w_done, n + 1)
                else:
                    dve.wait_ge(panel_used, p + 1)
                hk = h1[:, n, t0:t0 + w]
                nc.vector.scalar_tensor_tensor(hk, ps[(2 * n + c) % 8][:, :], gates[:, 1, n, 0:1], hk,
                                               ALU.mult, ALU.add).then_inc(w_res, 1)

    norm0 = Norm(0, 0, h0, nh0, nl0, ALL)
    ffn0 = Ffn("f0", 0, 0, h0, norm0, hidh0, hidl0, ALL, PANEL0)
    norm1 = Norm(3, 1, h0, nh0, nl0, ALL)
    win_p0 = ffn0.end_panel
    merge_p0 = win_p0 + len(win)
    norm2 = Norm(6, 2, h1, n1h, n1l, LAT)
    ffn1_p0 = merge_p0 + 2 * KT
    ffn1 = Ffn("f1", 1, 2, h1, norm2, hidh1, hidl1, LAT, ffn1_p0)
    norm3 = Norm(8, 0, h1, None, None, LAT, final=y_fin)

    def once(f):
        return lambda eng, c, k: f(eng) if (c, k) == (0, 0) else None

    block = stack.enter_context(nc.Block())

    @block.sync
    def _(sp):
        load_sp(sp)
        ffn0.sp(sp)
        win_sp(sp, win_p0, ffn0, norm1)
        gla_setup_sp(sp)
        gla_out_sp(sp)
        qk_sp(sp)
        merge_sp(sp, merge_p0)
        ffn1.sp(sp)
        result_sp(sp)

    @block.scalar
    def _(act):
        load_act(act)

        def ready0(act):
            act.wait_ge(turn_evac_v, 10)
            act.wait_ge(turn_evac_s, 10)
        norm0.act(act, once(ready0), early=True)
        ffn0.act(act)
        norm1.act(act, once(ffn0.wait_end))
        win_act(act, win_p0)
        gla_state_act(act)
        gla_intra_act(act)
        gla_out_act(act)
        qk_act(act)
        att_act(act)
        norm2.act(act, once(lambda a: a.wait_ge(w_res, 16)))
        ffn1.act(act)
        norm3.act(act, once(ffn1.wait_end))
        result_copy(act, 1, lambda o, i: nc.scalar.activation(o, i, ACT.Copy), fin_evac_s)

    @block.tensor
    def _(pe):
        pe.sem_inc(panel_used, PANEL0)
        load_pe(pe)
        mod_pe(pe, range(0, 2), ())
        norm0.early_pe(pe, lambda c: mod_pe(pe, (c + 2,), (c,)))
        mod_pe(pe, range(5, MOD_GROUP), range(3, MOD_GROUP))
        mod_pe(pe, range(MOD_GROUP, 2 * MOD_GROUP), range(MOD_GROUP, 2 * MOD_GROUP))
        ffn0.pe(pe)
        norm1.pe(pe)
        win_pe(pe, win_p0, norm1)
        gla_state_pe(pe, len(win_units))
        gla_intra_pe(pe)
        gla_out_pe(pe)
        qk_pe(pe)
        att_pe(pe)
        merge_pe(pe, merge_p0)
        norm2.pe(pe)
        ffn1.pe(pe)
        norm3.pe(pe)
        result_pe(pe, lambda pe, i: pe.wait_ge(norm3.scaled, norm3.u0 + KT * (1 + i // 4)) if i % 4 == 0 else None)

    @block.vector
    def _(dve):
        dve.sem_inc(panel_split, 2 * PANEL0)
        load_dve(dve)
        dve.wait_ge(turn_evac_s, 10)
        norm0.early_sums(dve, lambda c: mod_copy(dve, c))
        for n in range(3, MOD_GROUP):
            norm0.inverse(dve, n - 3)
            mod_copy(dve, n)
        mod_finish(dve, 0)
        due = {4: 6, 9: 7, 13: 8, 18: 9}
        norm0.dve(dve, lambda u: mod_copy(dve, due[u]) if u in due else None, early=True)
        split_panel(dve, pn(PANEL0))
        for n in range(MOD_GROUP + len(due), 2 * MOD_GROUP):
            mod_copy(dve, n)
        mod_finish(dve, 1)
        ffn0.dve(dve)
        ffn0.wait_end(dve)
        split_panel(dve, pn(win_p0))
        norm1.dve(dve)
        win_dve(dve, win_p0)
        dve.wait_ge(win_evac, len(win_units))
        gla_state_dve(dve)
        gla_intra_dve(dve)
        gla_out_dve(dve)
        qk_dve(dve)
        att_dve(dve)
        merge_dve(dve, merge_p0)
        dve.wait_ge(w_res, 16)
        split_panel(dve, pn(ffn1_p0))
        norm2.dve(dve)
        ffn1.dve(dve)
        ffn1.wait_end(dve)
        norm3.dve(dve)
        result_copy(dve, 0, lambda o, i: nc.vector.tensor_copy(o, i), fin_evac_v)

    stack.close()


_INS = ["x", "c", "ctx", "c_ctx", "w_mod", "b_mod", "g_norm", "w_ffn_up", "w_ffn_down", "w_in", "g_q", "g_k",
        "w_decay", "b_decay", "g_gla", "w_branch", "b_gate", "w_out", "g_final"]
_OUTS = [((1, SEQ, D), "float32")]


def kernel(**inputs):
    import numpy as _np
    import concourse.bacc as _bacc
    from concourse import mybir as _mybir
    from concourse.bass_utils import run_bass_kernel_spmd as _run

    nc = _bacc.Bacc("TRN2", target_bir_lowering=False, num_devices=1)
    arrays, args = {}, []
    given = {name: _np.ascontiguousarray(inputs[name]) for name in _INS}
    given["shape_consts"] = shape_constants()
    given["rope_tables"] = rope_tables()
    for name, a in given.items():
        arrays[f"in_{name}_dram"] = a
        args.append(nc.dram_tensor(f"in_{name}_dram", a.shape, _mybir.dt.from_np(a.dtype), kind="ExternalInput").ap())
    for i, (shape, dtype) in enumerate(_OUTS):
        dt = _mybir.dt.from_np(_np.dtype(dtype))
        args.append(nc.dram_tensor(f"out_{i}_dram", shape, dt, kind="ExternalOutput").ap())
    build(nc, *args)
    r = _run(nc, [arrays], core_ids=[0])
    got = tuple(r.results[0][f"out_{i}_dram"] for i in range(len(_OUTS)))
    return got[0]
```
